# Optimizing a Trainium2 kernel written in Bass

```python
import math
import jax, jax.numpy as jnp
from jax import lax
import numpy as np

D_MODEL = 1024
BATCH = 1
SEQ = 512
DEPTH = 1
DEC_BATCH = 1
DEC_SEQ = 1024
PAST_LEN = 128

ATT_HEADS = 4
ATT_QK_DIM = 64
ATT_V_DIM = 2 * ATT_QK_DIM
ATT_WIDTH = ATT_HEADS * ATT_V_DIM
Q_BLOCK = 128
HG_HEADS = 4
HG_K = 128
HG_V = 128
HG_WIDTH = HG_HEADS * HG_V
HG_CHUNK = 64
MIX_WIDTH = ATT_WIDTH + HG_WIDTH
IN_SPLITS = (ATT_HEADS * 2 * ATT_QK_DIM, ATT_HEADS * 2 * ATT_QK_DIM, ATT_WIDTH,
             HG_HEADS * HG_K, HG_HEADS * HG_K, HG_HEADS * HG_K, HG_WIDTH, HG_WIDTH)
IN_WIDTH = sum(IN_SPLITS)
N_EXPERTS = 16
EC_CAPACITY = 2
EXPERT_FF = 1024
EPS = 1e-6

kernel_name = 'hybrid_diffattn_hgrn2_ec_encoder'

def rms_norm(x, g):
    xf = x.astype(jnp.float32)
    y = xf * lax.rsqrt(jnp.mean(xf * xf, axis=-1, keepdims=True) + EPS)
    return (y * g.astype(jnp.float32)).astype(x.dtype)

def diff_attention(q, k, v, lam):
    B, T = q.shape[0], q.shape[1]
    nb = T // Q_BLOCK
    scale = ATT_QK_DIM ** -0.5
    slopes = 2.0 ** (-8.0 * (jnp.arange(ATT_HEADS, dtype=jnp.float32) + 1.0) / ATT_HEADS)
    qb = q.reshape(B, nb, Q_BLOCK, ATT_HEADS, 2, ATT_QK_DIM).transpose(1, 0, 3, 4, 2, 5)
    kt = k.transpose(0, 2, 3, 1, 4)
    vt = v.transpose(0, 2, 1, 3)
    kpos = jnp.arange(T, dtype=jnp.float32)

    def block(args):
        qblk, bi = args
        s = jnp.einsum('bhjqd,bhjkd->bhjqk', qblk, kt).astype(jnp.float32) * scale
        qpos = bi.astype(jnp.float32) * Q_BLOCK + jnp.arange(Q_BLOCK, dtype=jnp.float32)
        dist = jnp.abs(qpos[:, None] - kpos[None, :])
        s = s - (slopes[:, None, None] * dist[None])[None, :, None]
        p = jax.nn.softmax(s, axis=-1)
        w = (p[:, :, 0] - lam * p[:, :, 1]).astype(vt.dtype)
        return jnp.einsum('bhqk,bhkv->bhqv', w, vt)

    o = lax.map(block, (qb, jnp.arange(nb)))
    return o.transpose(1, 0, 3, 2, 4).reshape(B, T, ATT_HEADS, ATT_V_DIM)

def hgrn2_chunk_scan(q, k, v, logf):
    B, T, H, K = q.shape
    V = v.shape[-1]
    n = T // HG_CHUNK

    def to_chunks(a):
        return a.reshape(B, n, HG_CHUNK, H, a.shape[-1]).transpose(1, 0, 3, 2, 4).astype(jnp.float32)

    mask = jnp.tril(jnp.ones((HG_CHUNK, HG_CHUNK), dtype=bool))[:, :, None]

    def step(S, xs):
        qc, kc, vc, gc = xs
        b = jnp.cumsum(gc, axis=2)
        diff = b[:, :, :, None, :] - b[:, :, None, :, :]
        dec = jnp.exp(jnp.where(mask, diff, -jnp.inf))
        A = jnp.einsum('bhtk,bhsk,bhtsk->bhts', qc, kc, dec)
        o = jnp.einsum('bhts,bhsv->bhtv', A, vc) + jnp.einsum('bhtk,bhkv->bhtv', qc * jnp.exp(b), S)
        b_last = b[:, :, -1, :]
        S_new = jnp.exp(b_last)[..., None] * S + jnp.einsum(
            'bhsk,bhsv->bhkv', kc * jnp.exp(b_last[:, :, None, :] - b), vc)
        return S_new, o

    S0 = jnp.zeros((B, H, K, V), jnp.float32)
    _, o = lax.scan(step, S0, (to_chunks(q), to_chunks(k), to_chunks(v), to_chunks(logf)))
    return o.transpose(1, 0, 3, 2, 4).reshape(B, T, H, V)

def mixer(h, layer, w_in, lq1, lk1, lq2, lk2, subln_g, lb, hg_norm_g, w_out):
    B, T, _ = h.shape
    proj = h @ w_in
    aq, ak, av, hq, hff, hfb, hi, hg = jnp.split(proj, list(np.cumsum(IN_SPLITS)[:-1]), axis=-1)
    lam_init = 0.8 - 0.6 * math.exp(-0.3 * layer)
    lam = (jnp.exp(jnp.sum(lq1.astype(jnp.float32) * lk1.astype(jnp.float32)))
           - jnp.exp(jnp.sum(lq2.astype(jnp.float32) * lk2.astype(jnp.float32))) + lam_init)
    att = diff_attention(aq.reshape(B, T, ATT_HEADS, 2, ATT_QK_DIM),
                         ak.reshape(B, T, ATT_HEADS, 2, ATT_QK_DIM),
                         av.reshape(B, T, ATT_HEADS, ATT_V_DIM), lam)
    att = (rms_norm(att, subln_g) * (1.0 - lam_init)).reshape(B, T, ATT_WIDTH)
    shp = (B, T, HG_HEADS, HG_K)
    q = jax.nn.silu(hq.astype(jnp.float32)).reshape(shp)
    v = hi.astype(jnp.float32).reshape(B, T, HG_HEADS, HG_V)
    f_f = (lb[0] + (1.0 - lb[0]) * jax.nn.sigmoid(hff.astype(jnp.float32))).reshape(shp)
    f_b = (lb[1] + (1.0 - lb[1]) * jax.nn.sigmoid(hfb.astype(jnp.float32))).reshape(shp)
    o_f = hgrn2_chunk_scan(q, 1.0 - f_f, v, jnp.log(f_f))
    o_b = jnp.flip(hgrn2_chunk_scan(jnp.flip(q, 1), jnp.flip(1.0 - f_b, 1), jnp.flip(v, 1),
                                    jnp.flip(jnp.log(f_b), 1)), 1)
    hgo = rms_norm(o_f + o_b, hg_norm_g).reshape(B, T, HG_WIDTH)
    hgo = (hgo * jax.nn.silu(hg.astype(jnp.float32))).astype(h.dtype)
    return jnp.concatenate([att.astype(h.dtype), hgo], axis=-1) @ w_out

def expert_choice_ffn(h, w_router, w_gate, w_up, w_down):
    B, T, D = h.shape
    n_tok = B * T
    cap = max(1, EC_CAPACITY * n_tok // N_EXPERTS)
    flat = h.reshape(n_tok, D)
    aff = jax.nn.softmax((flat @ w_router).astype(jnp.float32), axis=-1)
    g, idx = lax.top_k(aff.T, cap)
    xs = flat[idx]
    hid = jax.nn.silu(jnp.einsum('ecd,edf->ecf', xs, w_gate)) * jnp.einsum('ecd,edf->ecf', xs, w_up)
    out = jnp.einsum('ecf,efd->ecd', hid, w_down) * g[..., None].astype(h.dtype)
    y = jnp.zeros((n_tok, D), h.dtype).at[idx.reshape(-1)].add(out.reshape(-1, D))
    return y.reshape(B, T, D)

def trunk(x, norm_mix_g, w_in, lambda_q1, lambda_k1, lambda_q2, lambda_k2, diff_subln_g,
          hgrn_lb, hgrn_norm_g, w_out, norm_ffn_g, w_router, w_gate, w_up, w_down, final_norm_g):
    lb_all = jnp.cumsum(jax.nn.softmax(hgrn_lb.astype(jnp.float32), axis=0), axis=0)
    lb_all = lb_all - lb_all[0]
    for layer in range(DEPTH):
        h = rms_norm(x, norm_mix_g[layer])
        x = x + mixer(h, layer, w_in[layer], lambda_q1[layer], lambda_k1[layer], lambda_q2[layer],
                      lambda_k2[layer], diff_subln_g[layer], lb_all[layer], hgrn_norm_g[layer], w_out[layer])
        h = rms_norm(x, norm_ffn_g[layer])
        x = x + expert_choice_ffn(h, w_router[layer], w_gate[layer], w_up[layer], w_down[layer])
    return rms_norm(x, final_norm_g)

def setup_inputs(seed: int = 0) -> dict:
    key = jax.random.key(seed)
    ks = jax.random.split(key, 20)
    nrm = jax.random.normal
    f32 = jnp.float32
    return {
        'x_prompt': nrm(ks[0], (BATCH, SEQ, D_MODEL), f32),
        'x_sample': nrm(ks[1], (DEC_BATCH, DEC_SEQ, D_MODEL), f32),
        'norm_mix_g': 1.0 + 0.02 * nrm(ks[2], (DEPTH, D_MODEL), f32),
        'w_in': nrm(ks[3], (DEPTH, D_MODEL, IN_WIDTH), f32) * D_MODEL ** -0.5,
        'lambda_q1': 0.1 * nrm(ks[4], (DEPTH, ATT_QK_DIM), f32),
        'lambda_k1': 0.1 * nrm(ks[5], (DEPTH, ATT_QK_DIM), f32),
        'lambda_q2': 0.1 * nrm(ks[6], (DEPTH, ATT_QK_DIM), f32),
        'lambda_k2': 0.1 * nrm(ks[7], (DEPTH, ATT_QK_DIM), f32),
        'diff_subln_g': 1.0 + 0.02 * nrm(ks[8], (DEPTH, ATT_V_DIM), f32),
        'hgrn_lb': 0.5 * nrm(ks[9], (DEPTH, 2, HG_HEADS * HG_K), f32),
        'hgrn_norm_g': 1.0 + 0.02 * nrm(ks[10], (DEPTH, HG_V), f32),
        'w_out': nrm(ks[11], (DEPTH, MIX_WIDTH, D_MODEL), f32) * MIX_WIDTH ** -0.5,
        'norm_ffn_g': 1.0 + 0.02 * nrm(ks[12], (DEPTH, D_MODEL), f32),
        'w_router': nrm(ks[13], (DEPTH, D_MODEL, N_EXPERTS), f32) * D_MODEL ** -0.5,
        'w_gate': nrm(ks[14], (DEPTH, N_EXPERTS, D_MODEL, EXPERT_FF), f32) * D_MODEL ** -0.5,
        'w_up': nrm(ks[15], (DEPTH, N_EXPERTS, D_MODEL, EXPERT_FF), f32) * D_MODEL ** -0.5,
        'w_down': nrm(ks[16], (DEPTH, N_EXPERTS, EXPERT_FF, D_MODEL), f32) * EXPERT_FF ** -0.5,
        'final_norm_g': 1.0 + 0.02 * nrm(ks[17], (D_MODEL,), f32),
    }

def reference(x_prompt, x_sample, norm_mix_g, w_in, lambda_q1, lambda_k1, lambda_q2, lambda_k2,
              diff_subln_g, hgrn_lb, hgrn_norm_g, w_out, norm_ffn_g, w_router, w_gate, w_up,
              w_down, final_norm_g):
    y_prompt = trunk(x_prompt, norm_mix_g, w_in, lambda_q1, lambda_k1, lambda_q2, lambda_k2,
                     diff_subln_g, hgrn_lb, hgrn_norm_g, w_out, norm_ffn_g, w_router, w_gate,
                     w_up, w_down, final_norm_g)
    y_sample = trunk(x_sample, norm_mix_g, w_in, lambda_q1, lambda_k1, lambda_q2, lambda_k2,
                     diff_subln_g, hgrn_lb, hgrn_norm_g, w_out, norm_ffn_g, w_router, w_gate,
                     w_up, w_down, final_norm_g)
    return (y_prompt, y_sample)


_drawn_inputs = setup_inputs


def setup_inputs(seed=0):
    import zlib

    import numpy as np

    out = dict(_drawn_inputs(seed))
    spreads = {}
    factors = {'lambda_k1': 3.092,
     'lambda_q2': 3.058,
     'diff_subln_g': 4.29,
     'hgrn_norm_g': 4.728,
     'norm_ffn_g': 4.133,
     'final_norm_g': 2.872}
    for name, (base, spread) in spreads.items():
        noise = np.random.default_rng([zlib.crc32(name.encode()), seed]).standard_normal(out[name].shape)
        drawn = base * np.exp(spread * noise) if base else spread * noise
        out[name] = __import__('jax').numpy.asarray(drawn.astype(out[name].dtype))
    for name, factor in factors.items():
        out[name] = (out[name] * factor).astype(out[name].dtype)
    return out
```

```python
from contextlib import ExitStack, contextmanager

import numpy as np

import concourse.bass as bass
from concourse import mybir

F32 = mybir.dt.float32
F32R = mybir.dt.float32r
I32 = mybir.dt.int32
U32 = mybir.dt.uint32
ALU = mybir.AluOpType
ACT = mybir.ActivationFunctionType
AX_X = mybir.AxisListType.X

P = 128
D = 1024
DT = D // P
BLK = 512
BC = BLK // P
HEADS = 4
QK = 64
T_SAMPLE, T_PROMPT = 1024, 512
N_TOK = T_SAMPLE + T_PROMPT
COL_AQ, COL_AK, COL_AV, COL_HQ, COL_HFF, COL_HFB, COL_HI, COL_HG = range(0, 8 * BLK, BLK)
HALF = DT // 2
EXPERTS = 16
FF = 1024
FT = FF // P
CAP_SAMPLE, CAP_PROMPT = 2 * T_SAMPLE // EXPERTS, 2 * T_PROMPT // EXPERTS
SLOTS = CAP_PROMPT + CAP_SAMPLE
EPS = 1e-6
LAM_INIT = 0.2
TOP = 8
PROMPT_ROW = 32
BIG = 3.0e38


def level_masks():
    s = np.arange(32)[:, None]
    t = np.arange(32)[None, :]
    m = np.zeros((32, 12, 32), np.float32)
    m[:, 0] = m[:, 6] = s == t
    for k in range(1, 6):
        half = 1 << (k - 1)
        pair = (s // (2 * half) == t // (2 * half)) & (s // half != t // half)
        m[:, k] = pair & (s < t)
        m[:, 6 + k] = pair & (s > t)
    return np.tile(m, (4, 1, 1))


def distances():
    p = np.arange(P)[:, None]
    u = np.arange(2 * T_SAMPLE - P)[None, :]
    return -np.abs(p + T_SAMPLE - P - u).astype(np.float32)


class Signal:

    def __init__(self, sem, per, ahead=True):
        self.sem, self.per = sem, per
        self.start = per if ahead else 0

    def at(self, i, k):
        return i * self.per + (self.start + k + 1)

    def last(self, i):
        return self.at(i, self.per - 1)


class Uses:

    def __init__(self, uses):
        self.uses = uses

    def before(self, i, name):
        n = [u[0] for u in self.uses].index(name)
        _, signal, k = self.uses[n - 1]
        return signal.sem, signal.at(i if n else i - 1, k)


@contextmanager
def semaphores(nc, prefix):
    made = []

    def sem(name):
        made.append(nc.alloc_semaphore(f"{prefix}_{name}"))
        return made[-1]

    yield sem
    nc.clear_and_free_semaphores(made)
    nc.all_engine_barrier()


class Carrier:

    def __init__(self, eng, cells, constant):
        self.eng, self.cells, self.constant, self.count = eng, cells, constant[:, 0:1], 0

    def __call__(self, part=slice(None)):
        n = self.count % self.cells.shape[-1]
        self.count += 1
        self.eng.tensor_tensor(self.cells[part, n:n + 1], self.constant[part, :], self.constant[part, :], ALU.add)


def start_signals(eng, signals):
    for s in signals:
        eng.sem_inc(s.sem, s.start)


def build(nc, x_s, x_p, g_mix, w_in, lq1, lk1, lq2, lk2, subln, lb_cols, hg_norm, w_out, g_ffn,
          w_router, w_gate, w_up, w_down, g_final, masks_in, dist_in, ident_in, out_p, out_s):
    h2_dram = nc.dram_tensor("h2_rows", (N_TOK, D), F32, kind="Internal").ap()
    y_dram = nc.dram_tensor("y_rows", (N_TOK, D), F32, kind="Internal").ap()

    with ExitStack() as whole:
        keep = lambda name, shape, dt=F32: whole.enter_context(nc.sbuf_tensor(name, shape, dt))
        psum = whole.enter_context(nc.psum_tensor("psum", [P, 8 * BLK], F32))
        banks = [psum[:, b * BLK:(b + 1) * BLK] for b in range(8)]
        ident = keep("ident", [P, P])
        aff = keep("aff", [48, T_SAMPLE])
        slope_cols = keep("slope_cols", [P, 2, HEADS])
        lb = keep("lb", [P, 2 * HEADS])
        one_minus_lb = keep("one_minus_lb", [P, 2 * HEADS])
        neg_lam = keep("neg_lam", [P, 1])
        att_g = keep("att_g", [P, 1])
        hg_g = keep("hg_g", [P, 1])
        minus_half = keep("minus_half", [P, BC])
        carriers = keep("carriers", [P, 8])
        carried = [carriers[:, 4 * e:4 * e + 4] for e in range(2)]

        with ExitStack() as mixer:
            constants(nc, mixer, ident, slope_cols, lb, one_minus_lb, neg_lam, att_g, hg_g, minus_half,
                      aff, lq1, lk1, lq2, lk2, subln, lb_cols, hg_norm, ident_in)
            mem = mixer_memory(nc, mixer)
            mem.pairs = [psum[:, 0:2 * BLK], psum[:, 2 * BLK:4 * BLK]]
            consts = (ident, slope_cols, lb, one_minus_lb, neg_lam, att_g, hg_g, carried, minus_half)
            for g, (x, T, row) in enumerate(((x_s, T_SAMPLE, 0), (x_p, T_PROMPT, T_SAMPLE))):
                normalise(nc, g, T, x, g_mix, ident, minus_half, banks, mem)
                hgrn(nc, g, T, w_in, masks_in, consts, banks, mem)
                attention(nc, g, T, w_in, dist_in, consts, banks, mem)
                project_out(nc, g, T, x, row, w_out, g_ffn, w_router, consts, banks, mem, aff,
                            h2_dram, y_dram)
        with ExitStack() as ffn:
            index_cols, gate_cols = choose(nc, ffn, ident, banks, aff)
            experts(nc, ffn, w_gate, w_up, w_down, ident, minus_half, psum, banks, index_cols, gate_cols, h2_dram, y_dram)
        finish(nc, g_final, minus_half, y_dram, out_p, out_s)


def constants(nc, ctx, ident, slope_cols, lb, one_minus_lb, neg_lam, att_g, hg_g, minus_half, aff,
              lq1, lk1, lq2, lk2, subln, lb_cols, hg_norm, ident_in):
    with ExitStack() as c:
        sem = c.enter_context(semaphores(nc, "k"))
        tmp = lambda name, shape: c.enter_context(nc.sbuf_tensor(name, shape, F32))
        lam_in = tmp("lam_in", [P, 4, QK])
        lam_prod = tmp("lam_prod", [P, 2, QK])
        lam_sum = tmp("lam_sum", [P, 2])
        lam_exp = tmp("lam_exp", [P, 2])
        lb_raw = tmp("lb_raw", [P, 2 * HEADS])
        lb_e = tmp("lb_e", [P, 2 * HEADS])
        lb_r = tmp("lb_r", [P, 2 * HEADS])
        loaded, chain, exps, filled = sem("loaded"), sem("const_chain"), sem("const_exps"), sem("filled")
        with nc.Block() as block:

            @block.sync
            def _(sp):
                sp.dma_start(ident[:], ident_in).then_inc(loaded, 16)
                for n, v in enumerate((lq1, lk1, lq2, lk2)):
                    sp.dma_start(lam_in[:, n, :], v[0].partition_broadcast(P)).then_inc(loaded, 16)
                sp.dma_start(lb_raw[:], lb_cols).then_inc(loaded, 16)
                sp.dma_start(att_g[:], subln.rearrange("o p -> p o")).then_inc(loaded, 16)
                sp.dma_start(hg_g[:], hg_norm.rearrange("o p -> p o")).then_inc(loaded, 16)
                sp.wait_ge(loaded, 8 * 16)

            @block.gpsimd
            def _(pool):
                for h in range(HEADS):
                    slope = 2.0 ** (-8.0 * (h + 1) / HEADS)
                    pool.memset(slope_cols[:, 0, h:h + 1], QK ** -0.5 / slope).then_inc(filled, 1)
                    pool.memset(slope_cols[:, 1, h:h + 1], -slope).then_inc(filled, 1)
                pool.memset(minus_half[:], -0.5).then_inc(filled, 1)
                pool.memset(aff[:], -1.0).then_inc(filled, 1)

            @block.scalar
            def _(act):
                act.wait_ge(chain, 3)
                act.activation(lam_exp[:], lam_sum[:], ACT.Exp).then_inc(exps, 1)
                act.activation(lb_e[:], lb_r[:], ACT.Exp).then_inc(exps, 1)

            @block.vector
            def _(dve):
                dve.wait_ge(loaded, 8 * 16)
                for n in range(2):
                    dve.tensor_tensor_reduce(out=lam_prod[:, n, :], in0=lam_in[:, 2 * n, :],
                                             in1=lam_in[:, 2 * n + 1, :], scale=1.0, scalar=0.0,
                                             op0=ALU.mult, op1=ALU.add,
                                             accum_out=lam_sum[:, n:n + 1]).then_inc(chain, 1)
                dve.tensor_tensor(lb_r[:], lb_raw[:], lb_raw[:], ALU.subtract).then_inc(chain, 1)
                dve.wait_ge(exps, 2)
                dve.scalar_tensor_tensor(neg_lam[:], lam_exp[:, 1:2], -LAM_INIT, lam_exp[:, 0:1],
                                         ALU.add, ALU.subtract).then_inc(chain, 1)
                dve.reciprocal(lb_r[:], lb_e[:]).then_inc(chain, 1)
                dve.tensor_scalar(att_g[:], att_g[:], 1.0 - LAM_INIT, None, ALU.mult).then_inc(chain, 1)
                dve.wait_ge(chain, 5)
                dve.tensor_tensor(lb_e[:], lb_e[:], lb_r[:], ALU.mult).then_inc(chain, 1)
                dve.wait_ge(chain, 7)
                dve.tensor_tensor(lb[:], lb_e[:], lb_e[:], ALU.subtract).then_inc(chain, 1)
                dve.wait_ge(chain, 8)
                dve.tensor_scalar(one_minus_lb[:], lb[:], -1.0, 1.0, ALU.mult, ALU.add).then_inc(chain, 1)


class Memory:
    pass


def mixer_memory(nc, ctx):
    m = Memory()
    sb = lambda name, shape, dt=F32: ctx.enter_context(nc.sbuf_tensor(name, shape, dt))
    T = T_SAMPLE
    m.hT_hi = sb("hT_hi", [P, DT, T], F32R)
    m.hT_lo = sb("hT_lo", [P, DT, T], F32R)
    m.mixT = sb("mixT", [P, 2 * HEADS, T])
    m.land = [sb(f"land{n}", [P, T]) for n in range(5)]
    m.q = [sb(f"q_{d}", [P, T]) for d in "fb"]
    m.k = [sb(f"k_{d}", [P, T]) for d in "fb"]
    m.f1 = [sb(f"f1_{d}", [P, T]) for d in "fb"]
    m.fup = [sb(f"fup_{d}", [P, BLK]) for d in "fb"]
    m.fend = [sb(f"fend_{d}", [P, T // P]) for d in "fb"]
    m.v = sb("v_rows", [P, T // P, P])
    m.gate = sb("gate", [P, T])
    m.at = sb("at", [P, T // P, P])
    m.state = [sb(f"state_{d}", [P, T // P, P]) for d in "fb"]
    m.k_rows = sb("k_rows", [P, T // P, P])
    m.diag = sb("diag", [P, BC, 32])
    m.masked = sb("masked", [P, 2, 12, 32])
    m.normed = sb("normed", [P, BC, P])
    m.masks = sb("masks", [P, 12, 32])
    m.w_raw = sb("w_raw", [P, 5, HALF, P])
    m.w_hi = sb("w_hi", [P, 2, HALF, P], F32R)
    m.w_lo = sb("w_lo", [P, 2, HALF, P], F32R)
    m.small = sb("small", [P, 8, 16])
    m.squares = sb("squares", [P, BC, P])
    m.dist = sb("dist", [P, 2 * T - P])
    return m


def normalise(nc, g, T, x, g_mix, ident, minus_half, banks, mem):
    NT = T // P
    with ExitStack() as c:
        sem = c.enter_context(semaphores(nc, f"n{g}"))
        x_in = [sem(f"x_in{s}") for s in range(2)]
        g_in, squared, powed, scaled, summed = sem("g_in"), sem("squared"), sem("powed"), sem("scaled"), sem("summed")
        turned, hi_done, lo_done = sem("turned"), sem("hi_done"), sem("lo_done")
        xt = [mem.land[0], mem.land[1]]
        h = [mem.q[0], mem.q[1]]
        junk = mem.k[0]
        g_row = mem.k[1]
        ss, ms, rstd = mem.small[:, 0, :], mem.small[:, 1, :], mem.small[:, 2, :]
        with nc.Block() as block:

            @block.sync
            def _(sp):
                sp.dma_start(g_row[:], g_mix[0].partition_broadcast(P)).then_inc(g_in, 16)
                for t in range(NT):
                    if t >= 2:
                        sp.wait_ge(scaled, t - 1)
                    sp.dma_start(xt[t % 2][:], x[t * P:(t + 1) * P, :]).then_inc(x_in[t % 2], 16)

            @block.scalar
            def _(act):
                for t in range(NT + 1):
                    if t < NT:
                        act.wait_ge(x_in[t % 2], 16 * (t // 2 + 1))
                        if t:
                            act.wait_ge(squared, t)
                        act.activation(junk[:], xt[t % 2][:], ACT.Square,
                                       accum_out=ss[:, t:t + 1]).then_inc(squared, 1)
                    if t:
                        for b in range(2):
                            act.wait_ge(turned, 2 * (t - 1) + b + 1)
                            act.copy(mem.hT_hi[:, 4 * b:4 * b + 4, (t - 1) * P:t * P],
                                     banks[2 * ((t - 1) % 2) + b][:].rearrange("p (n c) -> p n c", c=P)
                                     ).then_inc(hi_done, 1)

            @block.gpsimd
            def _(pool):
                for t in range(NT):
                    pool.wait_ge(summed, t + 1)
                    pool.tensor_tensor(rstd[:, t:t + 1], ms[:, t:t + 1], minus_half[:, 0:1],
                                       ALU.pow).then_inc(powed, 1)

            @block.vector
            def _(dve):
                def mean(t):
                    dve.wait_ge(squared, t + 1)
                    dve.tensor_scalar(ms[:, t:t + 1], ss[:, t:t + 1], 1.0 / D, EPS, ALU.mult,
                                      ALU.add).then_inc(summed, 1)

                dve.wait_ge(g_in, 16)
                mean(0)
                for t in range(NT + 1):
                    if t < NT:
                        if t + 1 < NT:
                            mean(t + 1)
                        dve.wait_ge(powed, t + 1)
                        if t >= 2:
                            dve.wait_ge(turned, 2 * (t - 1))
                        dve.scalar_tensor_tensor(h[t % 2][:], xt[t % 2][:], rstd[:, t:t + 1], g_row[:],
                                                 ALU.mult, ALU.mult).then_inc(scaled, 1)
                    if t:
                        for b in range(2):
                            dve.wait_ge(hi_done, 2 * (t - 1) + b + 1)
                            part = (slice(None), slice(4 * b, 4 * b + 4), slice((t - 1) * P, t * P))
                            dve.tensor_tensor(mem.hT_lo[part],
                                              banks[2 * ((t - 1) % 2) + b][:].rearrange("p (n c) -> p n c", c=P),
                                              mem.hT_hi[part].bitcast(F32), ALU.subtract).then_inc(lo_done, 1)

            @block.tensor
            def _(pe):
                for t in range(NT):
                    pe.wait_ge(scaled, t + 1)
                    for b in range(2):
                        if t >= 2:
                            pe.wait_ge(lo_done, 2 * (t - 2) + b + 1)
                        for n in range(4):
                            mm = pe.transpose(banks[2 * (t % 2) + b][:, n * P:(n + 1) * P],
                                              h[t % 2][:, (4 * b + n) * P:(4 * b + n + 1) * P], ident[:])
                        mm.then_inc(turned, 1)


class Projection:

    def __init__(self, sem, T, cols, ring, by_dve, banks, w_in, mem):
        self.cols, self.ring, self.mem, self.banks = cols, ring, mem, banks
        self.w = w_in.rearrange("(n p) c -> p n c", p=P)
        self.NB = T // BLK
        self.units = 2 * len(cols)
        self.by_dve = by_dve
        self.raw_in = [Signal(sem(f"w_in{s}"), 16 * (self.units // ring)) for s in range(ring)]
        self.hi = Signal(sem("w_hi"), self.units)
        self.lo = Signal(sem("w_lo"), self.units)
        self.summed = Signal(sem("summed"), self.units * self.NB)
        self.land_act = Signal(sem("land_act"), len(cols) * self.NB)
        self.land_dve = Signal(sem("land_dve"), max(1, len(by_dve) * self.NB))
        self.uses = []
        for k in range(2):
            uses = []
            for t in range(len(cols)):
                for b in range(self.NB):
                    if self.bank_of(t, b) == k:
                        if t in by_dve:
                            uses.append(((t, b), self.land_dve, by_dve.index(t) * self.NB + b))
                        else:
                            uses.append(((t, b), self.land_act, t * self.NB + b))
            self.uses.append(Uses(uses))

    def bank_of(self, tile, b):
        return b if self.NB == 2 else tile % 2

    def load(self, sp, j, column, u):
        part = self.w[:, (u % 2) * HALF:(u % 2 + 1) * HALF, self.cols[u // 2]:self.cols[u // 2] + BLK]
        src = part[:, :, 0:P] if column is None else part[:, :, P:][:, :, bass.ds(column, P)]
        sp.wait_ge(self.lo.sem, self.lo.at(j, u - self.ring))
        sp.dma_start(self.mem.w_raw[:, u % self.ring, :, :], src).then_inc(self.raw_in[u % self.ring].sem, 16)

    def split_hi(self, act, j, u):
        arrived = self.raw_in[u % self.ring]
        act.wait_ge(arrived.sem, arrived.at(j, 16 * (u // self.ring) + 15))
        act.wait_ge(self.summed.sem, self.summed.at(j, self.NB * (u - 1) - 1))
        act.copy(self.mem.w_hi[:, u % 2, :, :], self.mem.w_raw[:, u % self.ring, :, :]).then_inc(self.hi.sem, 1)

    def split_lo(self, dve, j, u):
        dve.wait_ge(self.hi.sem, self.hi.at(j, u))
        dve.tensor_tensor(self.mem.w_lo[:, u % 2, :, :], self.mem.w_raw[:, u % self.ring, :, :],
                          self.mem.w_hi[:, u % 2, :, :].bitcast(F32), ALU.subtract).then_inc(self.lo.sem, 1)

    def multiply(self, pe, j, u):
        tile, half = divmod(u, 2)
        mem = self.mem
        pe.wait_ge(self.lo.sem, self.lo.at(j, u))
        for b in range(self.NB):
            out = self.banks[self.bank_of(tile, b)]
            if half == 0:
                pe.wait_ge(*self.uses[self.bank_of(tile, b)].before(j, (tile, b)))
            for n in range(HALF):
                k = half * HALF + n
                hi, lo = mem.hT_hi[:, k, b * BLK:(b + 1) * BLK], mem.hT_lo[:, k, b * BLK:(b + 1) * BLK]
                pe.matmul(out[:], mem.w_hi[:, u % 2, n, :], hi, start=(k == 0), stop=False)
                pe.matmul(out[:], mem.w_hi[:, u % 2, n, :], lo, start=False, stop=False)
                mm = pe.matmul(out[:], mem.w_lo[:, u % 2, n, :], hi, start=False, stop=(k == DT - 1))
            mm.then_inc(self.summed.sem, 1)


def beside(slots, units):
    out, done = [], 0
    if units:
        out.append(("split", 0))
    for s, step in enumerate(slots):
        out.append(step)
        upto = units * (s + 1) // len(slots)
        for u in range(done, upto):
            if u + 1 < units:
                out.append(("split", u + 1))
            out.append(("unit", u))
            if u % 2:
                out.append(("land", u // 2))
        done = upto
    return out


def beside_at(slots, units):
    out = [("split", 0)]
    for step in slots:
        if step[0] == "unit":
            if step[1] + 1 < units:
                out.append(("split", step[1] + 1))
            out.append(step)
            if step[1] % 2:
                out.append(("land", step[1] // 2))
        else:
            out.append(step)
    return out


def run_heads(eng, body, first, both, last):
    for step in first:
        body(step, None, 0)
    with eng.Fori(0, HEADS - 1) as i:
        for step in both:
            body(step, i, i + 1)
    for step in last:
        body(step, HEADS - 1, None)


def hgrn(nc, g, T, w_in, masks_in, consts, banks, mem):
    NT, NB = T // P, T // BLK
    ident, slope_cols, lb, one_minus_lb, neg_lam, att_g, hg_g, carried, minus_half = consts
    with ExitStack() as c:
        sem = c.enter_context(semaphores(nc, f"h{g}"))
        X, FAR, TURN = banks[0:4], banks[4], banks[5]
        V, Q, FF_, FB, G = range(5)
        proj = Projection(sem, T, [COL_HI, COL_HQ, COL_HFF, COL_HFB, COL_HG], 5, [Q, G], banks[6:8], w_in, mem)
        mask_in = sem("mask_in")
        v_turned = Signal(sem("v_turned"), NB)
        level_read = [Signal(sem(f"level_{d}"), 8 * NB) for d in "fb"]
        k_turned = Signal(sem("k_turned"), 2 * NB)
        added = Signal(sem("added"), 2 * NB)
        o_summed = Signal(sem("o_summed"), NB)
        o_turned = Signal(sem("o_turned"), NB)
        v_rows = Signal(sem("v_rows"), NB)
        far_placed = Signal(sem("far_placed"), NB)
        k_rows = Signal(sem("k_rows"), 2 * NB)
        squared = Signal(sem("squared"), NB)
        gates = Signal(sem("gates"), 2)
        updated = [Signal(sem(f"updated_{d}"), 8 * NB) for d in "fb"]
        masked = Signal(sem("masked"), 4 * NB)
        summed_up = Signal(sem("summed_up"), 4 * NB)
        state = [Signal(sem(f"state_{d}"), NT - 1) for d in "fb"]
        mean = Signal(sem("mean"), NB)
        normed = Signal(sem("normed"), NB)
        mixed = Signal(sem("mixed"), NB)
        q_taken = Signal(sem("q_taken"), 2)
        k_made = Signal(sem("k_made"), 2)
        gate_taken = Signal(sem("gate_taken"), 1)
        placed = Signal(sem("placed"), 4 * NB)
        powed = Signal(sem("powed"), NB)

        kt_bank = lambda d, b: (2 * d + b) % 4
        ds_bank = lambda d, b: (2 * d + b + 1) % 4
        slots = [("start",)] + [("v_rows", b) for b in range(NB)]
        for b in range(NB):
            slots += [("level", b, k) for k in range(8)] + [("diag", b)]
        for d in range(2):
            slots += [("k_rows", d, b) for b in range(NB)]
            slots += [("state", d, b) for b in (range(NB) if d == 0 else reversed(range(NB)))]
        slots += [("o", b) for b in range(NB)]
        for b in range(NB):
            slots += [("norm", b), ("mix", b)]
        stages = beside([("none",)], proj.units), beside(slots, proj.units), slots
        in_order = [s for s in slots if s[0] == "state"]
        nth = lambda step: in_order.index(step)
        first_state = lambda b, n, d: (b * BC + n == 0) if d == 0 else (b * BC + n == NT - 1)

        x_uses = []
        for s in range(4):
            uses = []
            for step in slots:
                if step[0] == "level" and step[2] == 0:
                    uses.append((step, masked, BC * step[1] + s))
                if step[0] == "k_rows" and kt_bank(*step[1:]) == s:
                    uses.append((step, k_rows, NB * step[1] + step[2]))
                if step[0] == "state" and ds_bank(*step[1:]) == s:
                    d, b = step[1:]
                    done = min((b + 1) * BC, NT - 1) if d == 0 else min((NB - b) * BC, NT - 1)
                    uses.append((step, state[d], done - 1))
            x_uses.append(Uses(uses))
        far_uses = Uses([(("level", b, 6), far_placed, b) for b in range(NB)]
                        + [(("o", b), normed, b) for b in range(NB)])
        if NB == 2:
            far_uses = Uses([(("level", b, 6), far_placed, b) for b in range(NB)] + [(("o", 0), normed, 0)])
            x_uses[0].uses.append((("o", 1), normed, 1))
        o_bank = lambda b: FAR if b == 0 else X[0]
        o_uses = lambda b: far_uses if b == 0 else x_uses[0]
        turn_uses = Uses([(("v_rows", b), v_rows, b) for b in range(NB)] + [(("mix", b), mixed, b) for b in range(NB)])
        ss, ms, rstd = mem.small[:, 0, :], mem.small[:, 1, :], mem.small[:, 2, :]
        chunked = lambda bank: bank[:].rearrange("p (n c) -> p n c", c=P)

        def halves(tile, b, half):
            return tile[:, b * BLK:(b + 1) * BLK].rearrange("p (n a l) -> p n a l", a=2, l=half)

        def products(d, b, k):
            if k == 0:
                return mem.f1[d][:, b * BLK:(b + 1) * BLK]
            if k == 7:
                return mem.fend[d][:, b * BC:(b + 1) * BC]
            at = BLK - (BLK >> (k - 1))
            return mem.fup[d][:, at:at + (BLK >> k)]

        with nc.Block() as block:

            @block.sync
            def _(sp):
                start_signals(sp, proj.raw_in)
                sp.dma_start(mem.masks[:], masks_in).then_inc(mask_in, 16)
                for u in range(proj.units):
                    proj.load(sp, 0, None, u)
                with sp.Fori(0, HEADS - 1) as i:
                    column = sp.snap(i * P)
                    for u in range(proj.units):
                        proj.load(sp, i + 1, column, u)

            @block.tensor
            def _(pe):
                start_signals(pe, [proj.summed, v_turned, *level_read, k_turned, added, o_summed, o_turned])

                def body(step, i, j):
                    kind = step[0]
                    if kind == "unit":
                        proj.multiply(pe, j, step[1])
                    elif kind == "v_rows":
                        b = step[1]
                        pe.wait_ge(proj.land_act.sem, proj.land_act.at(i, NB * V + b))
                        pe.wait_ge(*turn_uses.before(i, step))
                        for n in range(BC):
                            at = b * BLK + n * P
                            mm = pe.transpose(TURN[:, n * P:(n + 1) * P], mem.land[V][:, at:at + P], ident[:])
                        mm.then_inc(v_turned.sem, 1)
                    elif kind == "level":
                        b, k = step[1:]
                        if k == 6:
                            pe.wait_ge(*far_uses.before(i, step))
                        for d in range(2):
                            if k == 0:
                                pe.wait_ge(q_taken.sem, q_taken.at(i, d))
                                pe.wait_ge(k_made.sem, k_made.at(i, d))
                            else:
                                pe.wait_ge(updated[d].sem, updated[d].at(i, 8 * b + k - 1))
                            q, kk = mem.q[d], mem.k[d]
                            for n in range(BC):
                                at = b * BLK + n * P
                                if k == 0 and d == 0:
                                    pe.wait_ge(*x_uses[n].before(i, step))
                                if k < 6:
                                    for z in range(0, P, 32):
                                        mm = pe.matmul(X[n][z:z + 32, (6 * d + k) * 32:(6 * d + k + 1) * 32],
                                                       kk[:, at + z:at + z + 32], q[:, at + z:at + z + 32],
                                                       start=True, stop=True, tile_position=(0, z))
                                elif k == 6:
                                    for z in range(0, P, 64):
                                        s, t = z + 32 * d, z + 32 * (1 - d)
                                        mm = pe.matmul(FAR[s:s + 32, n * 96:n * 96 + 32], kk[:, at + s:at + s + 32],
                                                       q[:, at + t:at + t + 32], start=True, stop=True,
                                                       tile_position=(0, s))
                                else:
                                    s, t = 64 * d, 64 * (1 - d)
                                    mm = pe.matmul(FAR[s:s + 64, n * 96 + 32:n * 96 + 96], kk[:, at + s:at + s + 64],
                                                   q[:, at + t:at + t + 64], start=True, stop=True,
                                                   tile_position=(0, s))
                            mm.then_inc(level_read[d].sem, 1)
                    elif kind == "k_rows":
                        d, b = step[1:]
                        bank, uses = X[kt_bank(d, b)], x_uses[kt_bank(d, b)]
                        pe.wait_ge(updated[d].sem, updated[d].at(i, 8 * b + 7))
                        pe.wait_ge(*uses.before(i, step))
                        for n in range(BC):
                            at = b * BLK + n * P
                            mm = pe.transpose(bank[:, n * P:(n + 1) * P], mem.k[d][:, at:at + P], ident[:])
                        mm.then_inc(k_turned.sem, 1)
                    elif kind == "state":
                        d, b = step[1:]
                        bank, uses = X[ds_bank(d, b)], x_uses[ds_bank(d, b)]
                        pe.wait_ge(k_rows.sem, k_rows.at(i, NB * d + b))
                        pe.wait_ge(v_rows.sem, v_rows.at(i, b))
                        pe.wait_ge(*uses.before(i, step))
                        for n in range(BC):
                            mm = pe.matmul(bank[:, n * P:(n + 1) * P], mem.k_rows[:, b * BC + n, :],
                                           mem.v[:, b * BC + n, :], start=True, stop=True)
                        mm.then_inc(added.sem, 1)
                    elif kind == "o":
                        b = step[1]
                        pe.wait_ge(placed.sem, placed.at(i, 4 * b + 3))
                        for d in range(2):
                            pe.wait_ge(state[d].sem, state[d].last(i))
                        if b == 0:
                            pe.wait_ge(far_placed.sem, far_placed.last(i))
                        else:
                            pe.wait_ge(*x_uses[0].before(i, step))
                        for n in range(BC):
                            w = b * BC + n
                            parts = [(mem.at[:, w, :], mem.v[:, w, :])]
                            if w > 0:
                                parts.append((mem.q[0][:, w * P:(w + 1) * P], mem.state[0][:, w, :]))
                            if w < NT - 1:
                                parts.append((mem.q[1][:, w * P:(w + 1) * P], mem.state[1][:, w, :]))
                            for m, (a, r) in enumerate(parts):
                                mm = pe.matmul(o_bank(b)[:, n * P:(n + 1) * P], a, r, start=(m == 0),
                                               stop=(m == len(parts) - 1))
                        mm.then_inc(o_summed.sem, 1)
                    elif kind == "mix":
                        b = step[1]
                        pe.wait_ge(normed.sem, normed.at(i, b))
                        pe.wait_ge(*turn_uses.before(i, step))
                        for n in range(BC):
                            mm = pe.transpose(TURN[:, n * P:(n + 1) * P], mem.normed[:, n, :], ident[:])
                        mm.then_inc(o_turned.sem, 1)

                run_heads(pe, body, *stages)

            @block.scalar
            def _(act):
                start_signals(act, [proj.hi, proj.land_act, v_rows, far_placed, k_rows, squared])
                taken = {V: v_turned, Q: q_taken, FF_: gates, FB: gates, G: gate_taken}

                def body(step, i, j):
                    kind = step[0]
                    if kind == "split":
                        proj.split_hi(act, j, step[1])
                    elif kind == "land":
                        n = step[1]
                        act.wait_ge(taken[n].sem, taken[n].last(j - 1))
                        for b in range(NB):
                            act.wait_ge(proj.summed.sem, proj.summed.at(j, (2 * n + 1) * NB + b))
                            act.activation(mem.land[n][:, b * BLK:(b + 1) * BLK], proj.banks[proj.bank_of(n, b)],
                                           ACT.Copy if n == V else ACT.Sigmoid).then_inc(proj.land_act.sem, 1)
                    elif kind == "v_rows":
                        b = step[1]
                        act.wait_ge(v_turned.sem, v_turned.at(i, b))
                        act.wait_ge(o_summed.sem, o_summed.last(i - 1))
                        act.copy(mem.v[:, b * BC:(b + 1) * BC, :], chunked(TURN)).then_inc(v_rows.sem, 1)
                    elif kind == "diag":
                        b = step[1]
                        act.wait_ge(o_summed.sem, o_summed.last(i - 1))
                        for d in range(2):
                            act.wait_ge(level_read[d].sem, level_read[d].at(i, 8 * b + 7))
                        far = FAR[:, 0:BC * 96].rearrange("p (n c) -> p n c", c=96)
                        at = mem.at[:, b * BC:(b + 1) * BC, :]
                        for z in range(0, P, 32):
                            t = z ^ 32
                            act.copy(at[z:z + 32, :, t:t + 32], far[z:z + 32, :, 0:32])
                        act.copy(at[0:64, :, 64:128], far[0:64, :, 32:96])
                        act.copy(at[64:128, :, 0:64], far[64:128, :, 32:96]).then_inc(far_placed.sem, 1)
                    elif kind == "k_rows":
                        d, b = step[1:]
                        act.wait_ge(k_turned.sem, k_turned.at(i, NB * d + b))
                        act.wait_ge(added.sem, added.at(i, NB * d - 1))
                        act.copy(mem.k_rows[:, b * BC:(b + 1) * BC, :], chunked(X[kt_bank(d, b)])).then_inc(k_rows.sem, 1)
                    elif kind == "norm":
                        b = step[1]
                        act.wait_ge(o_summed.sem, o_summed.at(i, b))
                        act.wait_ge(mean.sem, mean.at(i, b - 1))
                        act.wait_ge(squared.sem, squared.at(i, b - 1))
                        for n in range(BC):
                            sq = act.activation(mem.squares[:, n, :], o_bank(b)[:, n * P:(n + 1) * P], ACT.Square,
                                                accum_out=ss[:, n:n + 1])
                        sq.then_inc(squared.sem, 1)

                run_heads(act, body, *stages)

            @block.vector
            def _(dve):
                start_signals(dve, [proj.lo, proj.land_dve, gates, *updated, masked, summed_up, *state, mean,
                                    normed, mixed])
                dve.wait_ge(mask_in, 16)

                def level(d, b, k, i):
                    if k == 0:
                        q = mem.q[d][:, b * BLK:(b + 1) * BLK]
                        dve.tensor_tensor(q, q, products(d, b, 0), ALU.mult).then_inc(updated[d].sem, 1)
                        return
                    half = 1 << (k - 1)
                    n = BLK // (2 * half)
                    q, kk = halves(mem.q[d], b, half), halves(mem.k[d], b, half)
                    f = products(d, b, k - 1).rearrange("p (n a) -> p n a", a=2)
                    late, early = (1, 0) if d == 0 else (0, 1)
                    dve.tensor_tensor(products(d, b, k), f[:, :, 0], f[:, :, 1], ALU.mult)
                    dve.tensor_tensor(q[:, :, late, :], q[:, :, late, :],
                                      f[:, :, early:early + 1].to_broadcast([P, n, half]), ALU.mult)
                    dve.tensor_tensor(kk[:, :, early, :], kk[:, :, early, :],
                                      f[:, :, late:late + 1].to_broadcast([P, n, half]),
                                      ALU.mult).then_inc(updated[d].sem, 1)

                def body(step, i, j):
                    kind = step[0]
                    if kind == "split":
                        proj.split_lo(dve, j, step[1])
                    elif kind == "land" and step[1] in (Q, G):
                        n = step[1]
                        for b in range(NB):
                            dve.wait_ge(proj.land_act.sem, proj.land_act.at(j, NB * n + b))
                            part = mem.land[n][:, b * BLK:(b + 1) * BLK]
                            dve.tensor_tensor(part, proj.banks[proj.bank_of(n, b)][:], part,
                                              ALU.mult).then_inc(proj.land_dve.sem, 1)
                    elif kind == "start":
                        for d, n in enumerate((FF_, FB)):
                            dve.wait_ge(proj.land_act.sem, proj.land_act.at(i, NB * n + NB - 1))
                            dve.wait_ge(k_made.sem, k_made.last(i - 1))
                            dve.tensor_scalar(mem.f1[d][:, 0:T], mem.land[n][:, 0:T],
                                              one_minus_lb[:, bass.ds(i + d * HEADS, 1)],
                                              lb[:, bass.ds(i + d * HEADS, 1)], ALU.mult,
                                              ALU.add).then_inc(gates.sem, 1)
                    elif kind == "level":
                        b, k = step[1:]
                        for d in range(2):
                            dve.wait_ge(level_read[d].sem, level_read[d].at(i, 8 * b + k))
                            if k == 0:
                                dve.wait_ge(gates.sem, gates.at(i, d))
                            else:
                                dve.wait_ge(updated[d].sem, updated[d].at(i, 8 * b + k - 1))
                            level(d, b, k, i)
                    elif kind == "diag":
                        b = step[1]
                        for n in range(BC):
                            e = BC * b + n
                            dve.wait_ge(summed_up.sem, summed_up.at(i, e - 2))
                            dve.tensor_tensor(mem.masked[:, n % 2, :, :], X[n][:, 0:12 * 32].rearrange("p (k t) -> p k t", t=32),
                                              mem.masks[:], ALU.mult).then_inc(masked.sem, 1)
                            dve.wait_ge(masked.sem, masked.at(i, e))
                            if n == 0:
                                dve.wait_ge(placed.sem, placed.at(i, 4 * b - 1))
                            dve.tensor_reduce(mem.diag[:, n, :], mem.masked[:, n % 2, :, :].rearrange("p k t -> p t k"),
                                              AX_X, ALU.add).then_inc(summed_up.sem, 1)
                    elif kind == "state":
                        d, b = step[1:]
                        dve.wait_ge(added.sem, added.at(i, nth(step)))
                        dve.wait_ge(o_summed.sem, o_summed.last(i - 1))
                        add = X[ds_bank(d, b)]
                        for n in (range(BC) if d == 0 else reversed(range(BC))):
                            w = b * BC + n
                            event, to = (w, w + 1) if d == 0 else (NT - 1 - w, w - 1)
                            if event == NT - 1:
                                continue
                            if event == 0:
                                dve.tensor_copy(mem.state[d][:, to, :], add[:, n * P:(n + 1) * P]).then_inc(state[d].sem, 1)
                                continue
                            dve.wait_ge(state[d].sem, state[d].at(i, event - 1))
                            dve.scalar_tensor_tensor(mem.state[d][:, to, :], mem.state[d][:, w, :],
                                                     mem.fend[d][:, w:w + 1], add[:, n * P:(n + 1) * P],
                                                     ALU.mult, ALU.add).then_inc(state[d].sem, 1)
                    elif kind == "norm":
                        b = step[1]
                        dve.wait_ge(squared.sem, squared.at(i, b))
                        dve.wait_ge(powed.sem, powed.at(i, b - 1))
                        dve.tensor_scalar(ms[:, 0:BC], ss[:, 0:BC], 1.0 / P, EPS, ALU.mult, ALU.add).then_inc(mean.sem, 1)
                        dve.wait_ge(powed.sem, powed.at(i, b))
                        dve.wait_ge(o_turned.sem, o_turned.at(i, b - 1))
                        dve.tensor_tensor(mem.normed[:], chunked(o_bank(b)),
                                          rstd[:, 0:BC].unsqueeze(2).to_broadcast([P, BC, P]),
                                          ALU.mult).then_inc(normed.sem, 1)
                    elif kind == "mix":
                        b = step[1]
                        dve.wait_ge(o_turned.sem, o_turned.at(i, b))
                        dve.wait_ge(gate_taken.sem, gate_taken.at(i, 0))
                        out = mem.mixT[:, bass.ds(i + HEADS, 1), b * BLK:(b + 1) * BLK]
                        dve.scalar_tensor_tensor(out, TURN[:].unsqueeze(1), hg_g[:, 0:1],
                                                 mem.gate[:, b * BLK:(b + 1) * BLK].unsqueeze(1),
                                                 ALU.mult, ALU.mult).then_inc(mixed.sem, 1)

                run_heads(dve, body, *stages)

            @block.gpsimd
            def _(pool):
                start_signals(pool, [q_taken, k_made, gate_taken, placed, powed])
                carry = Carrier(pool, carried[1], minus_half)

                def body(step, i, j):
                    kind = step[0]
                    if kind == "start":
                        pool.wait_ge(o_summed.sem, o_summed.last(i - 1))
                        pool.wait_ge(proj.land_dve.sem, proj.land_dve.at(i, NB - 1))
                        carry()
                        for d in range(2):
                            pool.tensor_copy(mem.q[d][:, 0:T], mem.land[Q][:, 0:T]).then_inc(q_taken.sem, 1)
                            pool.wait_ge(gates.sem, gates.at(i, d))
                            carry()
                            pool.tensor_scalar(mem.k[d][:, 0:T], mem.f1[d][:, 0:T], -1.0, 1.0, ALU.mult,
                                               ALU.add).then_inc(k_made.sem, 1)
                        pool.wait_ge(proj.land_dve.sem, proj.land_dve.at(i, 2 * NB - 1))
                        pool.wait_ge(mixed.sem, mixed.last(i - 1))
                        carry()
                        pool.tensor_copy(mem.gate[:, 0:T], mem.land[G][:, 0:T]).then_inc(gate_taken.sem, 1)
                    elif kind == "diag":
                        b = step[1]
                        pool.wait_ge(summed_up.sem, summed_up.at(i, BC * b + BC - 1))
                        pool.wait_ge(gate_taken.sem, gate_taken.at(i, 0))
                        for n, z in enumerate(range(0, P, 32)):
                            pool.wait_ge(placed.sem, placed.at(i, 4 * b + n - 1))
                            carry(slice(z, z + 32))
                            pool.tensor_copy(mem.at[z:z + 32, b * BC:(b + 1) * BC, z:z + 32],
                                             mem.diag[z:z + 32, :, :]).then_inc(placed.sem, 1)
                    elif kind == "norm":
                        b = step[1]
                        pool.wait_ge(placed.sem, placed.last(i))
                        pool.wait_ge(mean.sem, mean.at(i, b))
                        pool.wait_ge(normed.sem, normed.at(i, b - 1))
                        pool.tensor_tensor(rstd[:, 0:BC], ms[:, 0:BC], minus_half[:, 0:BC], ALU.pow).then_inc(powed.sem, 1)

                run_heads(pool, body, *stages)


def attention(nc, g, T, w_in, dist_in, consts, banks, mem):
    NT, NB = T // P, T // BLK
    ident, slope_cols, lb, one_minus_lb, neg_lam, att_g, hg_g, carried, minus_half = consts
    with ExitStack() as c:
        sem = c.enter_context(semaphores(nc, f"a{g}"))
        TURN, OUT = banks[4], banks[5]
        Q, K, V = range(3)
        proj = Projection(sem, T, [COL_AQ, COL_AK, COL_AV], 3, [], banks[6:8], w_in, mem)
        dist_ready = sem("dist_ready")
        v_turned = Signal(sem("v_turned"), NB)
        scored = Signal(sem("scored"), 2 * NT)
        w_turned = Signal(sem("w_turned"), NT * NB)
        summed = Signal(sem("o_summed"), NT)
        o_turned = Signal(sem("o_turned"), NB)
        v_rows = Signal(sem("v_rows"), NB)
        exped = Signal(sem("exped"), 2 * NT)
        w_rows = Signal(sem("w_rows"), NT * NB)
        squared = Signal(sem("squared"), NB)
        slopes = Signal(sem("slopes"), 1)
        biased = Signal(sem("biased"), 2 * NT)
        ratio = Signal(sem("ratio"), 3 * NT)
        weighed = Signal(sem("weighed"), NT)
        scales = Signal(sem("scales"), 4 * NB)
        rescaled = Signal(sem("rescaled"), NB)
        normed = Signal(sem("normed"), NB)
        mixed = Signal(sem("mixed"), NB)
        taken = Signal(sem("taken"), 2)
        powed = Signal(sem("powed"), NB)

        slots = [(kind, 0, m) for m in range(2) for kind in ("scores", "exp")] + [("v_rows", b) for b in range(NB)]
        for t in range(NT + 1):
            if t == NT:
                slots.append(("unit", 4))
            if t:
                slots.append(("turn", t - 1, 0))
            if t + 1 < NT:
                slots.append(("scores", t + 1, 0))
            if t and NB == 2:
                slots.append(("turn", t - 1, 1))
            if t + 1 < NT:
                slots += [("exp", t + 1, 0), ("scores", t + 1, 1), ("exp", t + 1, 1)]
            if t == NT - 1:
                slots.append(("take",))
            if t < NT:
                slots.append(("weigh", t))
            slots += [("unit", u) for u in range(4) if u * (NT - 2) // 3 == t]
            if t:
                slots.append(("out", t - 1))
                if t > BC and t % BC == 1:
                    slots.append(("mix", t // BC - 1))
                if t % BC == 0:
                    slots.append(("norm", t // BC - 1))
        slots += [("unit", 5), ("mix", NB - 1)]
        alone = [s for s in slots if s[0] not in ("unit", "take")]
        stages = beside_at([("unit", u) for u in range(4)] + [("take",)] + [("unit", 4), ("unit", 5)], proj.units), \
            beside_at(slots, proj.units), alone

        def score_banks(t, j):
            return banks[2 * j:2 * j + 2] if NB == 2 else [banks[2 * j + t % 2]]

        turn_uses = []
        for step in slots:
            if step[0] == "v_rows":
                turn_uses.append((step, v_rows, step[1]))
            if step[0] == "turn":
                turn_uses.append((step, w_rows, NB * step[1] + step[2]))
            if step[0] == "mix":
                turn_uses.append((step, mixed, step[1]))
        turn_uses = Uses(turn_uses)
        chunked = lambda bank: bank[:].rearrange("p (n c) -> p n c", c=P)
        small = mem.small
        row_sum, cross = small[:, 0:2, :], small[:, 2, :]
        low = small[:, 3, :]
        ss, ms, rstd, inv = small[:, 4, :], small[:, 5, :], small[:, 6, :], small[:, 7, :]
        q_now, k_now = mem.gate, mem.at[:].rearrange("p n c -> p (n c)")
        scores = [mem.k[0], mem.k[1]]
        probs = [[mem.q[0], mem.q[1]], [mem.f1[0], mem.f1[1]]]
        weights = [mem.state[0][:].rearrange("p n c -> p (n c)"), mem.state[1][:].rearrange("p n c -> p (n c)")]
        w_keys = mem.k_rows
        slope_now = small[:, 0, 15:16]

        with nc.Block() as block:

            @block.sync
            def _(sp):
                start_signals(sp, proj.raw_in)
                sp.dma_start(mem.dist[:], dist_in).then_inc(dist_ready, 16)
                for u in range(proj.units):
                    proj.load(sp, 0, None, u)
                with sp.Fori(0, HEADS - 1) as i:
                    column = sp.snap(i * P)
                    for u in range(proj.units):
                        proj.load(sp, i + 1, column, u)

            @block.tensor
            def _(pe):
                start_signals(pe, [proj.summed, v_turned, scored, w_turned, summed, o_turned])

                def body(step, i, j):
                    kind = step[0]
                    if kind == "unit":
                        proj.multiply(pe, j, step[1])
                    elif kind == "v_rows":
                        b = step[1]
                        pe.wait_ge(proj.land_act.sem, proj.land_act.at(i, NB * V + b))
                        pe.wait_ge(*turn_uses.before(i, step))
                        for n in range(BC):
                            at = b * BLK + n * P
                            mm = pe.transpose(TURN[:, n * P:(n + 1) * P], mem.land[V][:, at:at + P], ident[:])
                        mm.then_inc(v_turned.sem, 1)
                    elif kind == "scores":
                        t, m = step[1:]
                        pe.wait_ge(taken.sem, taken.at(i, 1))
                        pe.wait_ge(biased.sem, biased.at(i, 2 * (t - 3 + NB) + m))
                        for b, bank in enumerate(score_banks(t, m)):
                            mm = pe.matmul(bank[:], q_now[QK * m:QK * (m + 1), t * P:(t + 1) * P],
                                           k_now[QK * m:QK * (m + 1), b * BLK:(b + 1) * BLK],
                                           start=True, stop=True)
                        mm.then_inc(scored.sem, 1)
                    elif kind == "turn":
                        t, b = step[1:]
                        pe.wait_ge(weighed.sem, weighed.at(i, t))
                        pe.wait_ge(*turn_uses.before(i, step))
                        for n in range(BC):
                            at = b * BLK + n * P
                            mm = pe.transpose(TURN[:, n * P:(n + 1) * P], weights[t % 2][:, at:at + P], ident[:])
                        mm.then_inc(w_turned.sem, 1)
                    elif kind == "out":
                        t = step[1]
                        pe.wait_ge(w_rows.sem, w_rows.at(i, NB * t + NB - 1))
                        pe.wait_ge(v_rows.sem, v_rows.last(i))
                        if t % BC == 0:
                            pe.wait_ge(normed.sem, normed.at(i, t // BC - 1))
                        for n in range(NT):
                            mm = pe.matmul(OUT[:, (t % BC) * P:(t % BC + 1) * P], w_keys[:, n, :], mem.v[:, n, :],
                                           start=(n == 0), stop=(n == NT - 1))
                        mm.then_inc(summed.sem, 1)
                    elif kind == "mix":
                        b = step[1]
                        pe.wait_ge(normed.sem, normed.at(i, b))
                        pe.wait_ge(*turn_uses.before(i, step))
                        for n in range(BC):
                            mm = pe.transpose(TURN[:, n * P:(n + 1) * P], mem.normed[:, n, :], ident[:])
                        mm.then_inc(o_turned.sem, 1)

                run_heads(pe, body, *stages)

            @block.scalar
            def _(act):
                start_signals(act, [proj.hi, proj.land_act, v_rows, exped, w_rows, squared])

                def body(step, i, j):
                    kind = step[0]
                    if kind == "split":
                        proj.split_hi(act, j, step[1])
                    elif kind == "land":
                        n = step[1]
                        if n == V:
                            act.wait_ge(v_turned.sem, v_turned.last(j - 1))
                        else:
                            act.wait_ge(taken.sem, taken.last(j - 1))
                        for b in range(NB):
                            act.wait_ge(proj.summed.sem, proj.summed.at(j, (2 * n + 1) * NB + b))
                            to, of = mem.land[n][:, b * BLK:(b + 1) * BLK], proj.banks[proj.bank_of(n, b)]
                            act.copy(to, of).then_inc(proj.land_act.sem, 1)
                    elif kind == "v_rows":
                        b = step[1]
                        act.wait_ge(v_turned.sem, v_turned.at(i, b))
                        act.wait_ge(summed.sem, summed.last(i - 1))
                        act.copy(mem.v[:, b * BC:(b + 1) * BC, :], chunked(TURN)).then_inc(v_rows.sem, 1)
                    elif kind == "exp":
                        t, m = step[1:]
                        act.wait_ge(weighed.sem, weighed.at(i, t - 2))
                        act.wait_ge(biased.sem, biased.at(i, 2 * t + m))
                        act.activation(probs[t % 2][m][:, 0:T], scores[m][:, 0:T], ACT.Exp, scale=-1.0,
                                       bias=low[:, m:m + 1], accum_out=row_sum[:, m, t % BC:t % BC + 1]
                                       ).then_inc(exped.sem, 1)
                    elif kind == "turn":
                        t, b = step[1:]
                        act.wait_ge(w_turned.sem, w_turned.at(i, NB * t + b))
                        act.wait_ge(summed.sem, summed.at(i, t - 1))
                        act.copy(w_keys[:, b * BC:(b + 1) * BC, :], chunked(TURN)).then_inc(w_rows.sem, 1)
                    elif kind == "norm":
                        b = step[1]
                        act.wait_ge(summed.sem, summed.at(i, BC * b + BC - 1))
                        act.wait_ge(scales.sem, scales.at(i, 4 * b - 1))
                        for n in range(BC):
                            sq = act.activation(mem.squares[:, n, :], OUT[:, n * P:(n + 1) * P], ACT.Square,
                                                accum_out=ss[:, n:n + 1])
                        sq.then_inc(squared.sem, 1)

                run_heads(act, body, *stages)

            @block.vector
            def _(dve):
                carry = Carrier(dve, carried[0], minus_half)
                start_signals(dve, [proj.lo, slopes, taken, biased, ratio, weighed, scales, rescaled, normed, mixed])
                dve.wait_ge(dist_ready, 16)

                def body(step, i, j):
                    kind = step[0]
                    if kind == "split":
                        proj.split_lo(dve, j, step[1])
                    elif kind == "take":
                        dve.wait_ge(scored.sem, scored.last(j - 1))
                        dve.wait_ge(proj.land_act.sem, proj.land_act.at(j, NB * K + NB - 1))
                        dve.tensor_scalar(q_now[:, 0:T], mem.land[Q][:, 0:T], slope_cols[:, 0, bass.ds(j, 1)], None,
                                          ALU.mult).then_inc(taken.sem, 1)
                        dve.tensor_copy(k_now[:, 0:T], mem.land[K][:, 0:T]).then_inc(taken.sem, 1)
                        dve.tensor_copy(slope_now, slope_cols[:, 1, bass.ds(j, 1)]).then_inc(slopes.sem, 1)
                        dve.wait_ge(slopes.sem, slopes.at(j, 0))
                    elif kind == "scores":
                        t, m = step[1:]
                        dve.wait_ge(scored.sem, scored.at(i, 2 * t + m))
                        dve.wait_ge(exped.sem, exped.at(i, 2 * (t - 1) + m))
                        carry()
                        at = T_SAMPLE - P - t * P
                        psum = mem.pairs[m][:, 0:T] if NB == 2 else score_banks(t, m)[0][:]
                        dve.tensor_tensor_reduce(out=scores[m][:, 0:T], in0=psum, in1=mem.dist[:, at:at + T],
                                                 scale=slope_now, scalar=BIG, op0=ALU.add, op1=ALU.min,
                                                 accum_out=low[:, m:m + 1]).then_inc(biased.sem, 1)
                    elif kind == "weigh":
                        t = step[1]
                        dve.wait_ge(exped.sem, exped.at(i, 2 * t + 1))
                        dve.wait_ge(weighed.sem, weighed.at(i, t - 1))
                        q = t % BC
                        if t == 0:
                            dve.wait_ge(scales.sem, scales.last(i - 1))
                        dve.reciprocal(cross[:, 0:1], row_sum[:, 1, q:q + 1]).then_inc(ratio.sem, 1)
                        dve.tensor_copy(inv[:, 4 + t:5 + t], row_sum[:, 0, q:q + 1]).then_inc(ratio.sem, 1)
                        dve.wait_ge(ratio.sem, ratio.at(i, 3 * t + 1))
                        dve.tensor_scalar(cross[:, 1:2], cross[:, 0:1], row_sum[:, 0, q:q + 1], neg_lam[:, 0:1],
                                          ALU.mult, ALU.mult).then_inc(ratio.sem, 1)
                        dve.wait_ge(ratio.sem, ratio.at(i, 3 * t + 2))
                        dve.wait_ge(w_turned.sem, w_turned.at(i, NB * (t - 2) + NB - 1))
                        dve.scalar_tensor_tensor(weights[t % 2][:, 0:T], probs[t % 2][1][:, 0:T], cross[:, 1:2],
                                                 probs[t % 2][0][:, 0:T], ALU.mult, ALU.add).then_inc(weighed.sem, 1)
                    elif kind == "norm":
                        b = step[1]
                        dve.wait_ge(ratio.sem, ratio.at(i, 3 * (BC * b + BC - 1) + 2))
                        dve.reciprocal(inv[:, 0:BC], inv[:, 4 + BC * b:4 + BC * (b + 1)]).then_inc(scales.sem, 1)
                        dve.wait_ge(scales.sem, scales.at(i, 4 * b))
                        dve.wait_ge(squared.sem, squared.at(i, b))
                        dve.wait_ge(powed.sem, powed.at(i, b - 1))
                        dve.tensor_tensor(ms[:, 0:BC], ss[:, 0:BC], inv[:, 0:BC], ALU.mult).then_inc(scales.sem, 1)
                        dve.wait_ge(scales.sem, scales.at(i, 4 * b + 1))
                        dve.tensor_tensor(ms[:, 4:4 + BC], ms[:, 0:BC], inv[:, 0:BC], ALU.mult).then_inc(scales.sem, 1)
                        dve.wait_ge(scales.sem, scales.at(i, 4 * b + 2))
                        dve.tensor_scalar(ms[:, 8:8 + BC], ms[:, 4:4 + BC], 1.0 / P, EPS, ALU.mult,
                                          ALU.add).then_inc(scales.sem, 1)
                        dve.wait_ge(powed.sem, powed.at(i, b))
                        dve.tensor_tensor(rstd[:, 4:4 + BC], rstd[:, 0:BC], inv[:, 0:BC], ALU.mult).then_inc(rescaled.sem, 1)
                        dve.wait_ge(rescaled.sem, rescaled.at(i, b))
                        dve.wait_ge(o_turned.sem, o_turned.at(i, b - 1))
                        dve.tensor_tensor(mem.normed[:], chunked(OUT),
                                          rstd[:, 4:4 + BC].unsqueeze(2).to_broadcast([P, BC, P]),
                                          ALU.mult).then_inc(normed.sem, 1)
                    elif kind == "mix":
                        b = step[1]
                        dve.wait_ge(o_turned.sem, o_turned.at(i, b))
                        out = mem.mixT[:, bass.ds(i, 1), b * BLK:(b + 1) * BLK]
                        dve.tensor_scalar(out, TURN[:].unsqueeze(1), att_g[:, 0:1], None, ALU.mult).then_inc(mixed.sem, 1)

                run_heads(dve, body, *stages)

            @block.gpsimd
            def _(pool):
                start_signals(pool, [powed])

                def body(step, i, j):
                    kind = step[0]
                    if kind == "norm":
                        b = step[1]
                        pool.wait_ge(scales.sem, scales.at(i, 4 * b + 3))
                        pool.wait_ge(normed.sem, normed.at(i, b - 1))
                        pool.tensor_tensor(rstd[:, 0:BC], ms[:, 8:8 + BC], minus_half[:, 0:BC], ALU.pow).then_inc(powed.sem, 1)

                run_heads(pool, body, *stages)


def project_out(nc, g, T, x, row, w_out, g_ffn, w_router, consts, banks, mem, aff, h2_dram, y_dram):
    NT = T // P
    ident, minus_half = consts[0], consts[-1]
    with ExitStack() as c:
        sem = c.enter_context(semaphores(nc, f"o{g}"))
        w_in = [sem(f"w_in{s}") for s in range(4)]
        x_in = [sem(f"x_in{s}") for s in range(2)]
        g_in, r_in = sem("g_in"), sem("r_in")
        w_hi, w_lo = sem("w_hi"), sem("w_lo")
        m_hi, m_lo, m_used = sem("m_hi"), sem("m_lo"), sem("m_used")
        added, squared, mean, powed, normed = sem("added"), sem("squared"), sem("mean"), sem("powed"), sem("normed")
        y_out, h_out = [sem(f"y_out{s}") for s in range(2)], [sem(f"h_out{s}") for s in range(2)]
        turned, h_turned, logits = sem("turned"), sem("h_turned"), sem("logits")
        highest, exped, inverse, shares, shares_turned, placed = (sem(s) for s in ("highest", "exped", "inverse", "shares", "shares_turned", "placed"))
        raw = mem.land[0:4]
        xr, x1, h2 = mem.q, mem.k, mem.f1
        g_row = mem.gate
        h2T = mem.state[0]
        router = mem.masks[:].rearrange("p a b -> p (a b)")[:, 0:DT * EXPERTS].rearrange("p (n e) -> p n e", e=EXPERTS)
        small = mem.small
        ss, ms, rstd, top, total, inv = (small[:, n, :] for n in range(6))
        e_row, a_row = small[:, 6, :], small[:, 7, :]
        rows = aff[0:16, :] if row == 0 else aff[PROMPT_ROW:PROMPT_ROW + 16, :]
        chunked = lambda bank: bank[:].rearrange("p (n c) -> p n c", c=P)
        with nc.Block() as block:

            @block.sync
            def _(sp):
                sp.dma_start(g_row[:], g_ffn[0].partition_broadcast(P)).then_inc(g_in, 16)
                sp.dma_start(router, w_router).then_inc(r_in, 16)
                for k in range(DT):
                    if k >= 4:
                        sp.wait_ge(w_lo, k - 3)
                    sp.dma_start(raw[k % 4][:], w_out[0, k * P:(k + 1) * P, :]).then_inc(w_in[k % 4], 16)
                for t in range(NT + 1):
                    if t < NT:
                        if t >= 2:
                            sp.wait_ge(added, 2 * (t - 1))
                        sp.dma_start(xr[t % 2][:], x[t * P:(t + 1) * P, :]).then_inc(x_in[t % 2], 16)
                    if t:
                        at = row + (t - 1) * P
                        sp.wait_ge(added, 2 * t)
                        sp.dma_start(y_dram[at:at + P, :], x1[(t - 1) % 2][:]).then_inc(y_out[(t - 1) % 2], 16)
                        sp.wait_ge(normed, t)
                        sp.dma_start(h2_dram[at:at + P, :], h2[(t - 1) % 2][:]).then_inc(h_out[(t - 1) % 2], 16)
                for s in range(2):
                    sp.wait_ge(y_out[s], 16 * (NT // 2))
                    sp.wait_ge(h_out[s], 16 * (NT // 2))

            @block.tensor
            def _(pe):
                def transposes(t):
                    pe.wait_ge(normed, t + 1)
                    for b in range(2):
                        if t:
                            pe.wait_ge(h_turned, 2 * (t - 1) + b + 1)
                        for n in range(4):
                            at = (4 * b + n) * P
                            mm = pe.transpose(banks[4 + b][:, n * P:(n + 1) * P], h2[t % 2][:, at:at + P], ident[:])
                        mm.then_inc(turned, 1)

                def route(t):
                    pe.wait_ge(h_turned, 2 * (t + 1))
                    if t:
                        pe.wait_ge(exped, t)
                    for n in range(DT):
                        mm = pe.matmul(banks[6][:, 0:EXPERTS], h2T[:, n, :], router[:, n, :], start=(n == 0),
                                       stop=(n == DT - 1))
                    mm.then_inc(logits, 1)

                def turn_shares(t):
                    pe.wait_ge(shares, t + 1)
                    if t:
                        pe.wait_ge(placed, t)
                    pe.transpose(banks[7][0:EXPERTS, 0:P], a_row, ident[:]).then_inc(shares_turned, 1)

                pe.wait_ge(r_in, 16)
                for t in range(NT + 1):
                    if t < NT:
                        if t >= 2:
                            pe.wait_ge(added, 2 * (t - 1))
                        for half in range(2):
                            u = 2 * t + half
                            pe.wait_ge(m_lo, u + 1)
                            for n in range(HALF):
                                k = half * HALF + n
                                if t == 0:
                                    pe.wait_ge(w_lo, k + 1)
                                for h in range(2):
                                    out = banks[2 * (t % 2) + h][:]
                                    hi, lo = (w[:, k, h * BLK:(h + 1) * BLK] for w in (mem.hT_hi, mem.hT_lo))
                                    pe.matmul(out, mem.w_hi[:, u % 2, n, :], hi, start=(k == 0), stop=False)
                                    pe.matmul(out, mem.w_hi[:, u % 2, n, :], lo, start=False, stop=False)
                                    mm = pe.matmul(out, mem.w_lo[:, u % 2, n, :], hi, start=False, stop=(k == DT - 1))
                            mm.then_inc(m_used, 1)
                            if t and half == 0:
                                transposes(t - 1)
                        if t:
                            route(t - 1)
                    else:
                        transposes(t - 1)
                        route(t - 1)
                    if t >= 2:
                        turn_shares(t - 2)
                turn_shares(NT - 1)

            @block.scalar
            def _(act):
                def split(u):
                    if u >= 2:
                        act.wait_ge(m_used, u - 1)
                    t, half = divmod(u, 2)
                    act.copy(mem.w_hi[:, u % 2, :, :], mem.mixT[:, half * HALF:(half + 1) * HALF, t * P:(t + 1) * P]).then_inc(m_hi, 1)

                def square(t):
                    act.wait_ge(added, 2 * t + 2)
                    if t:
                        act.wait_ge(squared, t)
                    act.activation(mem.land[4][:], x1[t % 2][:], ACT.Square, accum_out=ss[:, t:t + 1]).then_inc(squared, 1)

                def take_turned(t):
                    for b in range(2):
                        act.wait_ge(turned, 2 * t + b + 1)
                        if t:
                            act.wait_ge(logits, t)
                        act.copy(h2T[:, 4 * b:4 * b + 4, :], chunked(banks[4 + b])).then_inc(h_turned, 1)

                def exps(t):
                    act.wait_ge(highest, t + 1)
                    if t:
                        act.wait_ge(shares, t)
                    act.activation(e_row, banks[6][:, 0:EXPERTS], ACT.Exp, bias=top[:, t:t + 1],
                                   accum_out=total[:, t:t + 1]).then_inc(exped, 1)

                def place(t):
                    act.wait_ge(shares_turned, t + 1)
                    act.copy(rows[:, t * P:(t + 1) * P], banks[7][0:EXPERTS, 0:P]).then_inc(placed, 1)

                split(0)
                split(1)
                for k in range(DT):
                    act.wait_ge(w_in[k % 4], 16 * (k // 4 + 1))
                    act.copy(mem.hT_hi[:, k, :], raw[k % 4][:]).then_inc(w_hi, 1)
                for t in range(NT + 1):
                    for u in range(2 * t + 2, min(2 * t + 4, 2 * NT)):
                        split(u)
                    if t:
                        take_turned(t - 1)
                    if t < NT:
                        square(t)
                    if t:
                        exps(t - 1)
                    if t >= 2:
                        place(t - 2)
                place(NT - 1)

            @block.gpsimd
            def _(pool):
                for t in range(NT):
                    pool.wait_ge(mean, t + 1)
                    pool.tensor_tensor(rstd[:, t:t + 1], ms[:, t:t + 1], minus_half[:, 0:1], ALU.pow).then_inc(powed, 1)

            @block.vector
            def _(dve):
                def split(u):
                    dve.wait_ge(m_hi, u + 1)
                    t, half = divmod(u, 2)
                    dve.tensor_tensor(mem.w_lo[:, u % 2, :, :], mem.mixT[:, half * HALF:(half + 1) * HALF, t * P:(t + 1) * P],
                                      mem.w_hi[:, u % 2, :, :].bitcast(F32), ALU.subtract).then_inc(m_lo, 1)

                def rows_of(t):
                    dve.wait_ge(x_in[t % 2], 16 * (t // 2 + 1))
                    dve.wait_ge(m_used, 2 * t + 2)
                    if t >= 2:
                        dve.wait_ge(y_out[t % 2], 16 * (t // 2))
                        dve.wait_ge(squared, t - 1)
                    for h in range(2):
                        part = slice(h * BLK, (h + 1) * BLK)
                        dve.tensor_tensor(x1[t % 2][:, part], banks[2 * (t % 2) + h][:], xr[t % 2][:, part],
                                          ALU.add).then_inc(added, 1)

                def norm(t):
                    dve.wait_ge(squared, t + 1)
                    dve.tensor_scalar(ms[:, t:t + 1], ss[:, t:t + 1], 1.0 / D, EPS, ALU.mult, ALU.add).then_inc(mean, 1)
                    dve.wait_ge(powed, t + 1)
                    if t >= 2:
                        dve.wait_ge(h_out[t % 2], 16 * (t // 2))
                        dve.wait_ge(turned, 2 * (t - 1))
                    dve.scalar_tensor_tensor(h2[t % 2][:], x1[t % 2][:], rstd[:, t:t + 1], g_row[:], ALU.mult,
                                             ALU.mult).then_inc(normed, 1)

                def tail(t):
                    dve.wait_ge(logits, t + 1)
                    dve.tensor_reduce(top[:, t:t + 1], banks[6][:, 0:EXPERTS], AX_X, ALU.max, negate=True).then_inc(highest, 1)
                    dve.wait_ge(exped, t + 1)
                    dve.reciprocal(inv[:, t:t + 1], total[:, t:t + 1]).then_inc(inverse, 1)
                    dve.wait_ge(inverse, t + 1)
                    if t:
                        dve.wait_ge(shares_turned, t)
                    dve.tensor_scalar(a_row, e_row, inv[:, t:t + 1], None, ALU.mult).then_inc(shares, 1)

                dve.wait_ge(g_in, 16)
                split(0)
                split(1)
                for k in range(DT):
                    dve.wait_ge(w_hi, k + 1)
                    dve.tensor_tensor(mem.hT_lo[:, k, :], raw[k % 4][:], mem.hT_hi[:, k, :].bitcast(F32),
                                      ALU.subtract).then_inc(w_lo, 1)
                for t in range(NT + 1):
                    for u in range(2 * t + 2, min(2 * t + 4, 2 * NT)):
                        split(u)
                    if t < NT:
                        rows_of(t)
                        norm(t)
                    if t:
                        tail(t - 1)


def choose(nc, ctx, ident, banks, aff):
    index_cols = ctx.enter_context(nc.sbuf_tensor("index_cols", [P, 2, EXPERTS], I32))
    gate_cols = ctx.enter_context(nc.sbuf_tensor("gate_cols", [P, 2, EXPERTS], F32))
    with ExitStack() as c:
        sem = c.enter_context(semaphores(nc, "c"))
        sb = lambda name, shape, dt=F32: c.enter_context(nc.sbuf_tensor(name, shape, dt))
        shares, index, index_f = sb("top_shares", [48, P]), sb("top_index", [48, P], U32), sb("index_f", [48, P])
        found, turned, taken = sem("found"), sem("turned"), sem("taken")
        rounds = CAP_SAMPLE // TOP
        with nc.Block() as block:

            @block.vector
            def _(dve):
                for r in range(rounds):
                    eight = slice(r * TOP, (r + 1) * TOP)
                    if r:
                        dve.wait_ge(found, 3 * r)
                    dve.max(shares[:, eight], aff[:]).then_inc(found, 1)
                    dve.wait_ge(found, 3 * r + 1)
                    dve.max_index(index[:, eight], shares[:, eight], aff[:]).then_inc(found, 1)
                    dve.wait_ge(found, 3 * r + 2)
                    dve.match_replace(aff[:], shares[:, eight], aff[:], -2.0).then_inc(found, 1)
                dve.wait_ge(found, 3 * rounds)
                dve.tensor_copy(index_f[:], index[:]).then_inc(found, 1)
                dve.tensor_copy(shares[PROMPT_ROW:48, CAP_PROMPT:P], shares[PROMPT_ROW:48, 0:CAP_PROMPT]).then_inc(found, 1)
                dve.wait_ge(turned, 1)
                dve.tensor_scalar(index_cols[:, 0, :], banks[0][:, PROMPT_ROW:PROMPT_ROW + EXPERTS],
                                  float(T_SAMPLE), None, ALU.add).then_inc(taken, 1)
                dve.tensor_copy(index_cols[:, 1, :], banks[0][:, 0:EXPERTS]).then_inc(taken, 1)
                dve.tensor_copy(gate_cols[:, 0, :], banks[1][:, PROMPT_ROW:PROMPT_ROW + EXPERTS]).then_inc(taken, 1)
                dve.tensor_copy(gate_cols[:, 1, :], banks[1][:, 0:EXPERTS]).then_inc(taken, 1)

            @block.tensor
            def _(pe):
                pe.wait_ge(found, 3 * rounds + 2)
                pe.transpose(banks[0][:, 0:48], index_f[:], ident[0:48, 0:48])
                pe.transpose(banks[1][:, 0:48], shares[:], ident[0:48, 0:48]).then_inc(turned, 1)

    return index_cols, gate_cols


def experts(nc, ctx, w_gate, w_up, w_down, ident, minus_half, psum, banks, index_cols, gate_cols, h2_dram, y_dram):
    RAW, PARTS, PAIRS, UNITS = 8, 4, EXPERTS // 2, 3 * DT
    Q = DT // 2
    with ExitStack() as c:
        sem = c.enter_context(semaphores(nc, "e"))
        sb = lambda name, shape, dt=F32: c.enter_context(nc.sbuf_tensor(name, shape, dt))
        raw = sb("raw", [P, RAW, FF])
        w_hi, w_lo = sb("we_hi", [P, PARTS, FF], F32R), sb("we_lo", [P, PARTS, FF], F32R)
        rows_p, rows_s = sb("rows_p", [CAP_PROMPT, D]), sb("rows_s", [P, D])
        x_parts = sb("x_parts", [P, DT, 2, SLOTS], F32R)
        x_hi, x_lo = (x_parts[:, :, n, :] for n in range(2))
        hid_parts = sb("hid_parts", [P, FT, 2 * SLOTS], F32R)
        hid_both, hid_lo = hid_parts[:, :, 0:2 * CAP_PROMPT], hid_parts[:, :, CAP_PROMPT:CAP_PROMPT + SLOTS]
        hid_hi = {slice(0, CAP_PROMPT): hid_parts[:, :, 0:CAP_PROMPT],
                  slice(CAP_PROMPT, SLOTS): hid_parts[:, :, CAP_PROMPT + SLOTS:]}
        sample_slots = slice(CAP_PROMPT, SLOTS)
        silu, hid = sb("silu", [P, FT, SLOTS]), sb("hid", [P, FT, SLOTS])
        low_rows = sb("low_rows", [CAP_PROMPT, D])
        result_p, result_s = sb("result_p", [CAP_PROMPT, D]), sb("result_s", [P, D])
        carried_act = sb("carried_act", [P, 1])
        carried_pool = sb("carried_pool", [P, 6])
        index_p = sb("index_p", [CAP_PROMPT, 2], I32)
        index_s = sb("index_s", [P, 2], I32)

        raw_in = [Signal(sem(f"raw_in{s}"), 2 * 16 * UNITS // RAW) for s in range(RAW)]
        hi, lo = Signal(sem("hi"), 2 * UNITS), Signal(sem("lo"), 2 * UNITS)
        used = Signal(sem("used"), 2 * UNITS)
        turned = Signal(sem("turned"), 2 * 4)
        x_hi_made, x_lo_made = Signal(sem("x_hi_made"), 2 * 4), Signal(sem("x_lo_made"), 2 * 4)
        gate_first, up_first = Signal(sem("gate_first"), 2 * 4), Signal(sem("up_first"), 2 * 4)
        gate_sum, silued = Signal(sem("gate_sum"), 2 * 4), Signal(sem("silued"), 2 * 4)
        up_sum, product = Signal(sem("up_sum"), 2 * 4), Signal(sem("product"), 2 * 4)
        hid_hi_made, hid_lo_made = Signal(sem("hid_hi_made"), 2 * 4), Signal(sem("hid_lo_made"), 2 * 4)
        scaled_low, scaled_p, scaled_s = (Signal(sem(s), 2 * 2) for s in ("scaled_low", "scaled_p", "scaled_s"))
        indexed = Signal(sem("indexed"), 2 * 2)
        gathered = Signal(sem("gathered"), 2 * 32, ahead=False)
        scattered = Signal(sem("scattered"), 2 * 32, ahead=False)
        written = Signal(sem("written"), 2)

        def half(p, stage):
            first = (p + {"gate": 0, "up": 1, "down": 0, "turn": 1}[stage]) % 2
            return banks[4 * first:4 * first + 4]

        def pair_of_banks(p, stage, b):
            first = 4 * ((p + {"gate": 0, "up": 1}[stage]) % 2) + 2 * b
            both = psum[:, first * BLK:(first + 2) * BLK].rearrange("p (n c) -> p n c", c=BLK)
            return [both[:, :, part * SLOTS:(part + 1) * SLOTS] for part in range(2)]

        def next_of(i, p):
            return (i, 1) if p == 0 else (i + 1, 0)

        def pair_steps(i, last):
            out = []
            after = {Q - 1: ("gate", 0), Q: ("silu", 0), 2 * Q - 1: ("up", 0), 2 * Q: ("high", 0), 2 * Q + 1: ("low", 0),
                     3 * Q - 1: ("gate", 1), 3 * Q: ("silu", 1), 4 * Q - 1: ("up", 1), 4 * Q: ("high", 1), 4 * Q + 1: ("low", 1)}
            for p in range(2):
                for n in range(UNITS):
                    ahead = n + PARTS - 1
                    if ahead < UNITS:
                        out.append(("split", i, p, ahead))
                    elif not (last and p == 1):
                        out.append(("split", *next_of(i, p), ahead - UNITS))
                    out.append(("unit", i, p, n))
                    if n in after:
                        out.append((after[n][0], i, p, after[n][1]))
                    if n == 4 * Q + 2 and not (last and p == 1):
                        out.append(("turn", *next_of(i, p)))
                out.append(("result", i, p))
            return out

        def run(eng, body):
            body("gather", 0, 0)
            body("turn", 0, 0)
            body("gather", 0, 1)
            for n in range(PARTS - 1):
                body("split", 0, 0, n)
            with eng.Fori(0, PAIRS - 1) as i:
                for step in pair_steps(i, False):
                    body(*step)
            for step in pair_steps(PAIRS - 1, True):
                body(*step)

        pair_of_tiles = lambda bank: bank[:, 0:2 * SLOTS].rearrange("p (n c) -> p n c", c=SLOTS)

        with nc.Block() as block:

            @block.sync
            def _(sp):
                start_signals(sp, raw_in)

                def loads(i):
                    for p in range(2):
                        e = sp.snap(2 * i + p)
                        for n in range(UNITS):
                            sp.wait_ge(lo.sem, lo.at(i, p * UNITS + n - RAW))
                            s = n % RAW
                            if n < 4 * Q:
                                w, h = (w_gate, w_up)[n // Q % 2], n // (2 * Q)
                                at = (n % Q) * 2 * P
                                src = w[0, bass.ds(e, 1), at:at + 2 * P, h * BLK:(h + 1) * BLK].rearrange("e (a p) f -> p (e a) f", p=P)
                                to = raw[:, s, :].rearrange("p (a f) -> p a f", f=BLK)
                            else:
                                at = (n - 4 * Q) * P
                                src, to = w_down[0, bass.ds(e, 1), at:at + P, :].rearrange("e p f -> p e f"), raw[:, s:s + 1, :]
                            sp.dma_start(to, src).then_inc(raw_in[s].sem, 16)

                with sp.Fori(0, PAIRS) as i:
                    loads(i)

            @block.tensor
            def _(pe):
                start_signals(pe, [used, turned])

                def body(kind, i, p, n=None):
                    if kind == "turn":
                        pe.wait_ge(gathered.sem, gathered.at(i, 32 * p + 31))
                        pe.wait_ge(product.sem, product.at(i, 4 * p - 1))
                        for b, bank in enumerate(half((p - 1) % 2, "turn")):
                            for k in range(2):
                                at = (2 * b + k) * P
                                pe.transpose(bank[:, k * SLOTS + CAP_PROMPT:(k + 1) * SLOTS], rows_s[:, at:at + P], ident[:])
                                mm = pe.transpose(bank[:, k * SLOTS:k * SLOTS + CAP_PROMPT], rows_p[:, at:at + P],
                                                  ident[0:CAP_PROMPT, 0:CAP_PROMPT])
                            mm.then_inc(turned.sem, 1)
                    elif kind == "unit":
                        s = n % PARTS
                        pe.wait_ge(lo.sem, lo.at(i, p * UNITS + n))
                        if n < 4 * Q:
                            stage, h = ("gate", "up")[n // Q % 2], n // (2 * Q)
                            if n == 0:
                                pe.wait_ge(x_lo_made.sem, x_lo_made.at(i, 4 * p + 3))
                            elif n == Q:
                                pe.wait_ge(scaled_p.sem, scaled_p.at(i, 2 * p - 1))
                                pe.wait_ge(scaled_s.sem, scaled_s.at(i, 2 * p - 1))
                            elif n == 2 * Q:
                                pe.wait_ge(gate_sum.sem, gate_sum.at(i, 4 * p + 1))
                            elif n == 3 * Q:
                                pe.wait_ge(up_sum.sem, up_sum.at(i, 4 * p + 1))
                            for a in range(2):
                                k = 2 * (n % Q) + a
                                for m in range(HALF):
                                    at = slice(a * BLK + m * P, a * BLK + (m + 1) * P)
                                    out = half(p, stage)[m]
                                    pe.matmul(out[:, 0:2 * SLOTS], w_hi[:, s, at], x_parts[:, k, :, :], start=(k == 0),
                                              stop=False, skip_group_check=True)
                                    mm = pe.matmul(out[:, SLOTS:2 * SLOTS], w_lo[:, s, at], x_hi[:, k, :], start=False,
                                                   stop=(k == DT - 1), skip_group_check=True)
                        else:
                            k = n - 4 * Q
                            if k % 2 == 0:
                                pe.wait_ge(hid_lo_made.sem, hid_lo_made.at(i, 4 * p + k // 2))
                            if k == 0:
                                pe.wait_ge(gate_sum.sem, gate_sum.at(i, 4 * p + 3))
                            out = half(p, "down")
                            a, b = hid_hi[sample_slots][:, k, :], hid_lo[:, k, sample_slots]
                            both = hid_both[:, k, :]
                            for h in range(2):
                                u, v = (w[:, s, h * BLK:(h + 1) * BLK] for w in (w_hi, w_lo))
                                first, last = k == 0, k == FT - 1
                                pe.matmul(out[2 + h][:], a, u, start=first, stop=False)
                                pe.matmul(out[2 + h][:], a, v, start=False, stop=False)
                                pe.matmul(out[2 + h][:], b, u, start=False, stop=last)
                                pe.matmul(out[h][:], both, u, start=first, stop=False)
                                mm = pe.matmul(out[h][:], both, v, start=False, stop=last)
                        mm.then_inc(used.sem, 1)

                run(pe, body)

            @block.scalar
            def _(act):
                start_signals(act, [hi, x_hi_made, gate_first, up_first, silued, hid_hi_made, scaled_low, scaled_s])

                def body(kind, i, p, n=None):
                    if kind == "split":
                        s = n % RAW
                        act.wait_ge(raw_in[s].sem, raw_in[s].at(i, 16 * (p * (UNITS // RAW) + n // RAW) + 15))
                        act.wait_ge(used.sem, used.at(i, p * UNITS + n - PARTS))
                        act.copy(w_hi[:, n % PARTS, :], raw[:, s, :]).then_inc(hi.sem, 1)
                    elif kind == "turn":
                        act.wait_ge(used.sem, used.at(i, p * UNITS - FT - 1))
                        for b, bank in enumerate(half((p - 1) % 2, "turn")):
                            act.wait_ge(turned.sem, turned.at(i, 4 * p + b))
                            act.copy(x_hi[:, 2 * b:2 * b + 2, :], pair_of_tiles(bank)).then_inc(x_hi_made.sem, 1)
                    elif kind == "gate":
                        act.wait_ge(used.sem, used.at(i, p * UNITS + (2 * n + 1) * Q - 1))
                        for b in range(2):
                            e = 4 * p + 2 * n + b
                            act.wait_ge(product.sem, product.at(i, e - 4))
                            act.copy(silu[:, 2 * (e % 4):2 * (e % 4) + 2, :], pair_of_banks(p, "gate", b)[0]).then_inc(gate_first.sem, 1)
                    elif kind == "up":
                        act.wait_ge(used.sem, used.at(i, p * UNITS + (2 * n + 2) * Q - 1))
                        for b in range(2):
                            e = 4 * p + 2 * n + b
                            act.wait_ge(hid_lo_made.sem, hid_lo_made.at(i, e - 4))
                            act.copy(hid[:, 2 * (e % 4):2 * (e % 4) + 2, :], pair_of_banks(p, "up", b)[0]).then_inc(up_first.sem, 1)
                    elif kind == "silu":
                        for e in (4 * p + 2 * n, 4 * p + 2 * n + 1):
                            act.wait_ge(gate_sum.sem, gate_sum.at(i, e))
                            part = silu[:, 2 * (e % 4):2 * (e % 4) + 2, :]
                            act.activation(part, part, ACT.Silu).then_inc(silued.sem, 1)
                    elif kind == "high":
                        act.wait_ge(used.sem, used.at(i, p * UNITS - 1))
                        for e in (4 * p + 2 * n, 4 * p + 2 * n + 1):
                            part = (slice(None), slice(2 * (e % 4), 2 * (e % 4) + 2), slice(None))
                            act.wait_ge(product.sem, product.at(i, e))
                            for slots, to in hid_hi.items():
                                made = act.copy(to[part], hid[part][:, :, slots])
                            made.then_inc(hid_hi_made.sem, 1)
                    elif kind == "result":
                        act.wait_ge(used.sem, used.at(i, p * UNITS + UNITS - 1))
                        act.wait_ge(written.sem, written.at(i, p - 1))
                        act.copy(carried_act[:], minus_half[:, 0:1])
                        for h in range(2):
                            act.activation(low_rows[:, h * BLK:(h + 1) * BLK], half(p, "down")[h][CAP_PROMPT:P, :], ACT.Copy,
                                           scale=gate_cols[CAP_PROMPT:P, 0, bass.ds(2 * i + p, 1)]).then_inc(scaled_low.sem, 1)
                        for h in range(2):
                            act.activation(result_s[:, h * BLK:(h + 1) * BLK], half(p, "down")[2 + h][:], ACT.Copy,
                                           scale=gate_cols[:, 1, bass.ds(2 * i + p, 1)]).then_inc(scaled_s.sem, 1)

                run(act, body)

            @block.vector
            def _(dve):
                start_signals(dve, [lo, x_lo_made, gate_sum, up_sum, product, hid_lo_made, scaled_p])

                def body(kind, i, p, n=None):
                    if kind == "split":
                        dve.wait_ge(hi.sem, hi.at(i, p * UNITS + n))
                        dve.tensor_tensor(w_lo[:, n % PARTS, :], raw[:, n % RAW, :], w_hi[:, n % PARTS, :].bitcast(F32),
                                          ALU.subtract).then_inc(lo.sem, 1)
                    elif kind == "turn":
                        for b, bank in enumerate(half((p - 1) % 2, "turn")):
                            dve.wait_ge(x_hi_made.sem, x_hi_made.at(i, 4 * p + b))
                            dve.tensor_tensor(x_lo[:, 2 * b:2 * b + 2, :], pair_of_tiles(bank),
                                              x_hi[:, 2 * b:2 * b + 2, :].bitcast(F32), ALU.subtract).then_inc(x_lo_made.sem, 1)
                    elif kind == "gate":
                        for b in range(2):
                            e = 4 * p + 2 * n + b
                            part = silu[:, 2 * (e % 4):2 * (e % 4) + 2, :]
                            second = pair_of_banks(p, "gate", b)[1]
                            dve.wait_ge(gate_first.sem, gate_first.at(i, e))
                            dve.tensor_tensor(part, part, second, ALU.add).then_inc(gate_sum.sem, 1)
                    elif kind == "up":
                        for b in range(2):
                            e = 4 * p + 2 * n + b
                            part = hid[:, 2 * (e % 4):2 * (e % 4) + 2, :]
                            second = pair_of_banks(p, "up", b)[1]
                            dve.wait_ge(up_first.sem, up_first.at(i, e))
                            dve.tensor_tensor(part, part, second, ALU.add).then_inc(up_sum.sem, 1)
                        for b in range(2):
                            e = 4 * p + 2 * n + b
                            part = (slice(None), slice(2 * (e % 4), 2 * (e % 4) + 2), slice(None))
                            dve.wait_ge(up_sum.sem, up_sum.at(i, e))
                            dve.wait_ge(silued.sem, silued.at(i, e))
                            dve.tensor_tensor(hid[part], hid[part], silu[part], ALU.mult).then_inc(product.sem, 1)
                    elif kind == "low":
                        for e in (4 * p + 2 * n, 4 * p + 2 * n + 1):
                            part = (slice(None), slice(2 * (e % 4), 2 * (e % 4) + 2), slice(None))
                            dve.wait_ge(hid_hi_made.sem, hid_hi_made.at(i, e))
                            for slots, high in hid_hi.items():
                                made = dve.tensor_tensor(hid_lo[part][:, :, slots], hid[part][:, :, slots], high[part].bitcast(F32), ALU.subtract)
                            made.then_inc(hid_lo_made.sem, 1)
                    elif kind == "result":
                        for h in range(2):
                            dve.wait_ge(scaled_low.sem, scaled_low.at(i, 2 * p + h))
                            dve.scalar_tensor_tensor(result_p[:, h * BLK:(h + 1) * BLK], half(p, "down")[h][0:CAP_PROMPT, :],
                                                     gate_cols[0:CAP_PROMPT, 0, bass.ds(2 * i + p, 1)],
                                                     low_rows[:, h * BLK:(h + 1) * BLK], ALU.mult, ALU.add).then_inc(scaled_p.sem, 1)

                run(dve, body)

            @block.gpsimd
            def _(pool):
                start_signals(pool, [indexed, written])
                carry = Carrier(pool, carried_pool, minus_half)

                def body(kind, i, p, n=None):
                    if kind == "gather":
                        pool.wait_ge(turned.sem, turned.at(i, 4 * p - 1))
                        carry()
                        e = bass.ds(2 * i + p, 1)
                        pool.tensor_copy(index_p[:, p:p + 1], index_cols[0:CAP_PROMPT, 0, e]).then_inc(indexed.sem, 1)
                        pool.tensor_copy(index_s[:, p:p + 1], index_cols[:, 1, e]).then_inc(indexed.sem, 1)
                        pool.wait_ge(indexed.sem, indexed.at(i, 2 * p + 1))
                        carry()
                        for rows, index in ((rows_p, index_p), (rows_s, index_s)):
                            pool.indirect_dma_start(rows[:], None, h2_dram, bass.IndirectOffsetOnAxis(ap=index[:, p:p + 1], axis=0)
                                                    ).then_inc(gathered.sem, 16)
                    elif kind == "result":
                        pool.wait_ge(scaled_p.sem, scaled_p.at(i, 2 * p + 1))
                        pool.wait_ge(scaled_s.sem, scaled_s.at(i, 2 * p + 1))
                        carry()
                        for rows, index in ((result_p, index_p), (result_s, index_s)):
                            pool.indirect_dma_start(y_dram, bass.IndirectOffsetOnAxis(ap=index[:, p:p + 1], axis=0), rows[:], None,
                                                    compute_op=ALU.add).then_inc(scattered.sem, 16)
                        pool.wait_ge(scattered.sem, scattered.at(i, 32 * p + 31))
                        pool.sem_inc(written.sem, 1)

                def with_gathers(i, last):
                    for p in range(2):
                        body("result", i, p)
                        if not last:
                            body("gather", i + 1, p)

                body("gather", 0, 0)
                body("gather", 0, 1)
                with pool.Fori(0, PAIRS - 1) as i:
                    with_gathers(i, False)
                with_gathers(PAIRS - 1, True)


def finish(nc, g_final, minus_half, y_dram, out_p, out_s):
    NT = N_TOK // P
    SLOTS_Y = 4
    with ExitStack() as c:
        sem = c.enter_context(semaphores(nc, "f"))
        sb = lambda name, shape: c.enter_context(nc.sbuf_tensor(name, shape, F32))
        y, out, junk, g_row = sb("y", [P, SLOTS_Y, D]), sb("out", [P, SLOTS_Y, D]), sb("junk", [P, D]), sb("g_row", [P, D])
        ss, ms, rstd = sb("ss", [P, NT]), sb("ms", [P, NT]), sb("rstd", [P, NT])
        y_in, y_out = [sem(f"y_in{s}") for s in range(SLOTS_Y)], [sem(f"y_out{s}") for s in range(SLOTS_Y)]
        g_in, squared, mean, powed, normed = sem("g_in"), sem("squared"), sem("mean"), sem("powed"), sem("normed")
        with nc.Block() as block:

            @block.sync
            def _(sp):
                sp.dma_start(g_row[:], g_final.partition_broadcast(P)).then_inc(g_in, 16)
                for t in range(NT):
                    if t >= SLOTS_Y:
                        sp.wait_ge(normed, t - SLOTS_Y + 1)
                    sp.dma_start(y[:, t % SLOTS_Y, :], y_dram[t * P:(t + 1) * P, :]).then_inc(y_in[t % SLOTS_Y], 16)

            @block.scalar
            def _(act):
                def store(t):
                    to = out_s[t * P:(t + 1) * P, :] if t < T_SAMPLE // P else out_p[t * P - T_SAMPLE:(t + 1) * P - T_SAMPLE, :]
                    act.wait_ge(normed, t + 1)
                    act.dma_start(to, out[:, t % SLOTS_Y, :]).then_inc(y_out[t % SLOTS_Y], 16)

                for t in range(NT):
                    act.wait_ge(y_in[t % SLOTS_Y], 16 * (t // SLOTS_Y + 1))
                    if t:
                        act.wait_ge(squared, t)
                    act.activation(junk[:], y[:, t % SLOTS_Y, :], ACT.Square, accum_out=ss[:, t:t + 1]).then_inc(squared, 1)
                    if t >= 2:
                        store(t - 2)
                store(NT - 2)
                store(NT - 1)
                for s in range(SLOTS_Y):
                    act.wait_ge(y_out[s], 16 * (NT // SLOTS_Y))

            @block.gpsimd
            def _(pool):
                for t in range(NT):
                    pool.wait_ge(mean, t + 1)
                    pool.tensor_tensor(rstd[:, t:t + 1], ms[:, t:t + 1], minus_half[:, 0:1], ALU.pow).then_inc(powed, 1)

            @block.vector
            def _(dve):
                dve.wait_ge(g_in, 16)
                for t in range(NT):
                    dve.wait_ge(squared, t + 1)
                    dve.tensor_scalar(ms[:, t:t + 1], ss[:, t:t + 1], 1.0 / D, EPS, ALU.mult, ALU.add).then_inc(mean, 1)
                    dve.wait_ge(powed, t + 1)
                    if t >= SLOTS_Y:
                        dve.wait_ge(y_out[t % SLOTS_Y], 16 * (t // SLOTS_Y))
                    dve.scalar_tensor_tensor(out[:, t % SLOTS_Y, :], y[:, t % SLOTS_Y, :], rstd[:, t:t + 1], g_row[:],
                                             ALU.mult, ALU.mult).then_inc(normed, 1)


def kernel(**inputs):
    import concourse.bacc as bacc
    from concourse.bass_utils import run_bass_kernel_spmd

    a = {name: np.ascontiguousarray(v) for name, v in inputs.items()}
    arrays = {
        "x_s": a["x_sample"].reshape(T_SAMPLE, D), "x_p": a["x_prompt"].reshape(T_PROMPT, D),
        "g_mix": a["norm_mix_g"], "w_in": a["w_in"][0],
        "lq1": a["lambda_q1"], "lk1": a["lambda_k1"], "lq2": a["lambda_q2"], "lk2": a["lambda_k2"],
        "subln": a["diff_subln_g"],
        "lb_cols": np.ascontiguousarray(a["hgrn_lb"].reshape(2 * HEADS, P).T),
        "hg_norm": a["hgrn_norm_g"], "w_out": a["w_out"], "g_ffn": a["norm_ffn_g"],
        "w_router": np.ascontiguousarray(a["w_router"].reshape(DT, P, EXPERTS).transpose(1, 0, 2)),
        "w_gate": a["w_gate"], "w_up": a["w_up"], "w_down": a["w_down"], "g_final": a["final_norm_g"],
        "masks_in": level_masks(), "dist_in": distances(), "ident_in": np.eye(P, dtype=np.float32),
    }
    nc = bacc.Bacc("TRN2", target_bir_lowering=False, num_devices=1)
    args = {n: nc.dram_tensor(f"in_{n}", v.shape, mybir.dt.from_np(v.dtype), kind="ExternalInput").ap()
            for n, v in arrays.items()}
    out_p = nc.dram_tensor("out_prompt", (T_PROMPT, D), F32, kind="ExternalOutput").ap()
    out_s = nc.dram_tensor("out_sample", (T_SAMPLE, D), F32, kind="ExternalOutput").ap()
    build(nc, **args, out_p=out_p, out_s=out_s)
    r = run_bass_kernel_spmd(nc, [{f"in_{n}": v for n, v in arrays.items()}], core_ids=[0]).results[0]
    return r["out_prompt"].reshape(1, T_PROMPT, D), r["out_sample"].reshape(1, T_SAMPLE, D)
```

```python
from contextlib import ExitStack, contextmanager

import numpy as np

import concourse.bass as bass
from concourse import mybir

F32 = mybir.dt.float32
F32R = mybir.dt.float32r
I32 = mybir.dt.int32
U32 = mybir.dt.uint32
ALU = mybir.AluOpType
ACT = mybir.ActivationFunctionType
AX_X = mybir.AxisListType.X

P = 128
D = 1024
DT = D // P
BLK = 512
BC = BLK // P
HEADS = 4
QK = 64
T_SAMPLE, T_PROMPT = 1024, 512
N_TOK = T_SAMPLE + T_PROMPT
COL_AQ, COL_AK, COL_AV, COL_HQ, COL_HFF, COL_HFB, COL_HI, COL_HG = range(0, 8 * BLK, BLK)
HALF = DT // 2
CUTS = 2
EXPERTS = 16
FF = 1024
FT = FF // P
CAP_SAMPLE, CAP_PROMPT = 2 * T_SAMPLE // EXPERTS, 2 * T_PROMPT // EXPERTS
SLOTS = CAP_PROMPT + CAP_SAMPLE
EPS = 1e-6
LAM_INIT = 0.2
TOP = 8
CHOICES = 3 * CAP_SAMPLE // TOP
CHOICES_BEFORE = {"attention": (10, 16), "out": 28}
PROMPT_ROW = 32
BIG = 3.0e38


def level_masks():
    s = np.arange(32)[:, None]
    t = np.arange(32)[None, :]
    m = np.zeros((32, 12, 32), np.float32)
    m[:, 0] = m[:, 6] = s == t
    for k in range(1, 6):
        half = 1 << (k - 1)
        pair = (s // (2 * half) == t // (2 * half)) & (s // half != t // half)
        m[:, k] = pair & (s < t)
        m[:, 6 + k] = pair & (s > t)
    return np.tile(m, (4, 1, 1))


def distances():
    p = np.arange(P)[:, None]
    u = np.arange(2 * T_SAMPLE - P)[None, :]
    return -np.abs(p + T_SAMPLE - P - u).astype(np.float32)


class Signal:

    def __init__(self, sem, per, ahead=True):
        self.sem, self.per = sem, per
        self.start = per if ahead else 0

    def at(self, i, k):
        return i * self.per + (self.start + k + 1)

    def last(self, i):
        return self.at(i, self.per - 1)


class Uses:

    def __init__(self, uses):
        self.uses = uses

    def before(self, i, name):
        n = [u[0] for u in self.uses].index(name)
        _, signal, k = self.uses[n - 1]
        return signal.sem, signal.at(i if n else i - 1, k)


@contextmanager
def semaphores(nc, prefix):
    made = []

    def sem(name):
        made.append(nc.alloc_semaphore(f"{prefix}_{name}"))
        return made[-1]

    yield sem
    nc.clear_and_free_semaphores(made)
    nc.all_engine_barrier()


class Carrier:

    def __init__(self, eng, cells, constant):
        self.eng, self.cells, self.constant, self.count = eng, cells, constant[:, 0:1], 0

    def __call__(self, part=slice(None)):
        n = self.count % self.cells.shape[-1]
        self.count += 1
        self.eng.tensor_tensor(self.cells[part, n:n + 1], self.constant[part, :], self.constant[part, :], ALU.add)


class Rounds:

    def __init__(self, sem, table, shares, index):
        self.sem, self.table, self.shares, self.index = sem, table, shares, index

    def step(self, dve, n, column=None):
        r, what = divmod(n, 3)
        column = r * TOP if column is None else column
        eight, places = (t[:, column:column + TOP] for t in (self.shares, self.index))
        if n:
            dve.wait_ge(self.sem, n)
        if what == 0:
            dve.max(eight, self.table).then_inc(self.sem, 1)
        elif what == 1:
            dve.max_index(places, eight, self.table).then_inc(self.sem, 1)
        else:
            dve.match_replace(self.table, eight, self.table, -2.0).then_inc(self.sem, 1)


def start_signals(eng, signals):
    for s in signals:
        eng.sem_inc(s.sem, s.start)


def build(nc, x_s, x_p, g_mix, w_in, lq1, lk1, lq2, lk2, subln, lb_cols, hg_norm, w_out, g_ffn,
          w_router, w_gate, w_up, w_down, g_final, masks_in, dist_in, ident_in, out_p, out_s):
    h2_dram = nc.dram_tensor("h2_rows", (N_TOK, D), F32, kind="Internal").ap()
    y_dram = nc.dram_tensor("y_rows", (N_TOK, D), F32, kind="Internal").ap()

    with ExitStack() as whole:
        keep = lambda name, shape, dt=F32: whole.enter_context(nc.sbuf_tensor(name, shape, dt))
        psum = whole.enter_context(nc.psum_tensor("psum", [P, 8 * BLK], F32))
        banks = [psum[:, b * BLK:(b + 1) * BLK] for b in range(8)]
        ident = keep("ident", [P, P])
        aff = keep("aff", [48, T_SAMPLE])
        shares, index = keep("shares", [48, P]), keep("index", [48, P], U32)
        slope_cols = keep("slope_cols", [P, 2, HEADS])
        lb = keep("lb", [P, 2 * HEADS])
        one_minus_lb = keep("one_minus_lb", [P, 2 * HEADS])
        neg_lam = keep("neg_lam", [P, 1])
        att_g = keep("att_g", [P, 1])
        hg_g = keep("hg_g", [P, 1])
        minus_half = keep("minus_half", [P, BC])
        carriers = keep("carriers", [P, 8])
        carried = [carriers[:, 4 * e:4 * e + 4] for e in range(2)]

        choosing = whole.enter_context(semaphores(nc, "t"))
        chosen = Rounds(choosing("chosen"), aff[0:16, :], shares[0:16, :], index[0:16, :])
        with ExitStack() as mixer:
            constants(nc, mixer, ident, slope_cols, lb, one_minus_lb, neg_lam, att_g, hg_g, minus_half,
                      aff, shares, lq1, lk1, lq2, lk2, subln, lb_cols, hg_norm, ident_in)
            mem = mixer_memory(nc, mixer)
            mem.pairs = [psum[:, 0:2 * BLK], psum[:, 2 * BLK:4 * BLK]]
            consts = (ident, slope_cols, lb, one_minus_lb, neg_lam, att_g, hg_g, carried, minus_half)
            for g, (x, T, row) in enumerate(((x_s, T_SAMPLE, 0), (x_p, T_PROMPT, T_SAMPLE))):
                with ExitStack() as stage:
                    stage_memory(nc, stage, mem, f"h{g}")
                    normalise(nc, g, T, x, g_mix, ident, minus_half, banks, mem)
                    hgrn(nc, g, T, w_in, masks_in, consts, banks, mem, chosen)
                with ExitStack() as stage:
                    attention_memory(nc, stage, mem, f"a{g}")
                    attention(nc, g, T, w_in, dist_in, consts, banks, mem, chosen)
                with ExitStack() as stage:
                    stage_memory(nc, stage, mem, f"o{g}")
                    project_out(nc, g, T, x, row, w_out, g_ffn, w_router, consts, banks, mem, aff,
                                h2_dram, y_dram, chosen)
        with ExitStack() as ffn:
            index_cols, gate_cols = choose(nc, ffn, ident, banks, aff, shares, index)
            experts(nc, ffn, w_gate, w_up, w_down, ident, minus_half, psum, banks, index_cols, gate_cols, h2_dram, y_dram)
        finish(nc, g_final, minus_half, y_dram, out_p, out_s)


def constants(nc, ctx, ident, slope_cols, lb, one_minus_lb, neg_lam, att_g, hg_g, minus_half, aff, shares,
              lq1, lk1, lq2, lk2, subln, lb_cols, hg_norm, ident_in):
    with ExitStack() as c:
        sem = c.enter_context(semaphores(nc, "k"))
        tmp = lambda name, shape: c.enter_context(nc.sbuf_tensor(name, shape, F32))
        lam_in = tmp("lam_in", [P, 4, QK])
        lam_prod = tmp("lam_prod", [P, 2, QK])
        lam_sum = tmp("lam_sum", [P, 2])
        lam_exp = tmp("lam_exp", [P, 2])
        lb_raw = tmp("lb_raw", [P, 2 * HEADS])
        lb_e = tmp("lb_e", [P, 2 * HEADS])
        lb_r = tmp("lb_r", [P, 2 * HEADS])
        loaded, chain, exps, filled = sem("loaded"), sem("const_chain"), sem("const_exps"), sem("filled")
        with nc.Block() as block:

            @block.sync
            def _(sp):
                sp.dma_start(ident[:], ident_in).then_inc(loaded, 16)
                for n, v in enumerate((lq1, lk1, lq2, lk2)):
                    sp.dma_start(lam_in[:, n, :], v[0].partition_broadcast(P)).then_inc(loaded, 16)
                sp.dma_start(lb_raw[:], lb_cols).then_inc(loaded, 16)
                sp.dma_start(att_g[:], subln.rearrange("o p -> p o")).then_inc(loaded, 16)
                sp.dma_start(hg_g[:], hg_norm.rearrange("o p -> p o")).then_inc(loaded, 16)
                sp.wait_ge(loaded, 8 * 16)

            @block.gpsimd
            def _(pool):
                for h in range(HEADS):
                    slope = 2.0 ** (-8.0 * (h + 1) / HEADS)
                    pool.memset(slope_cols[:, 0, h:h + 1], QK ** -0.5 / slope).then_inc(filled, 1)
                    pool.memset(slope_cols[:, 1, h:h + 1], -slope).then_inc(filled, 1)
                pool.memset(minus_half[:], -0.5).then_inc(filled, 1)
                pool.memset(aff[:], -1.0).then_inc(filled, 1)
                pool.memset(shares[:], 0.0).then_inc(filled, 1)

            @block.scalar
            def _(act):
                act.wait_ge(chain, 3)
                act.activation(lam_exp[:], lam_sum[:], ACT.Exp).then_inc(exps, 1)
                act.activation(lb_e[:], lb_r[:], ACT.Exp).then_inc(exps, 1)

            @block.vector
            def _(dve):
                dve.wait_ge(loaded, 8 * 16)
                for n in range(2):
                    dve.tensor_tensor_reduce(out=lam_prod[:, n, :], in0=lam_in[:, 2 * n, :],
                                             in1=lam_in[:, 2 * n + 1, :], scale=1.0, scalar=0.0,
                                             op0=ALU.mult, op1=ALU.add,
                                             accum_out=lam_sum[:, n:n + 1]).then_inc(chain, 1)
                dve.tensor_tensor(lb_r[:], lb_raw[:], lb_raw[:], ALU.subtract).then_inc(chain, 1)
                dve.wait_ge(exps, 2)
                dve.scalar_tensor_tensor(neg_lam[:], lam_exp[:, 1:2], -LAM_INIT, lam_exp[:, 0:1],
                                         ALU.add, ALU.subtract).then_inc(chain, 1)
                dve.reciprocal(lb_r[:], lb_e[:]).then_inc(chain, 1)
                dve.tensor_scalar(att_g[:], att_g[:], 1.0 - LAM_INIT, None, ALU.mult).then_inc(chain, 1)
                dve.wait_ge(chain, 5)
                dve.tensor_tensor(lb_e[:], lb_e[:], lb_r[:], ALU.mult).then_inc(chain, 1)
                dve.wait_ge(chain, 7)
                dve.tensor_tensor(lb[:], lb_e[:], lb_e[:], ALU.subtract).then_inc(chain, 1)
                dve.wait_ge(chain, 8)
                dve.tensor_scalar(one_minus_lb[:], lb[:], -1.0, 1.0, ALU.mult, ALU.add).then_inc(chain, 1)


class Memory:
    pass


def mixer_memory(nc, ctx):
    m = Memory()
    sb = lambda name, shape, dt=F32: ctx.enter_context(nc.sbuf_tensor(name, shape, dt))
    T = T_SAMPLE
    m.hT_hi = sb("hT_hi", [P, DT, T], F32R)
    m.hT_lo = sb("hT_lo", [P, DT, T], F32R)
    m.mixT = sb("mixT", [P, 2 * HEADS, T])
    m.q = [sb(f"q_{d}", [P, T]) for d in "fb"]
    m.k = [sb(f"k_{d}", [P, T]) for d in "fb"]
    m.f1 = [sb(f"f1_{d}", [P, T]) for d in "fb"]
    m.v = sb("v_rows", [P, T // P, P])
    m.state = [sb(f"state_{d}", [P, T // P, P]) for d in "fb"]
    m.k_rows = sb("k_rows", [P, T // P, P])
    m.normed = sb("normed", [P, BC, P])
    m.w_hi = sb("w_hi", [P, 2, HALF, P], F32R)
    m.w_lo = sb("w_lo", [P, 2, HALF, P], F32R)
    m.small = sb("small", [P, 8, 16])
    return m


def stage_memory(nc, ctx, m, stage):
    sb = lambda name, shape: ctx.enter_context(nc.sbuf_tensor(f"{stage}_{name}", shape, F32))
    T = T_SAMPLE
    m.land = [sb(f"land{n}", [P, T]) for n in range(5)]
    m.w_raw = sb("w_raw", [P, 5, HALF, P])
    m.fup = [sb(f"fup_{d}", [P, BLK]) for d in "fb"]
    m.fend = [sb(f"fend_{d}", [P, T // P]) for d in "fb"]
    m.gate = sb("gate", [P, T])
    m.at = sb("at", [P, T // P, P])
    m.diag = sb("diag", [P, BC, 32])
    m.masked = sb("masked", [P, 2, 12, 32])
    m.masks = sb("masks", [P, 12, 32])


def attention_memory(nc, ctx, m, stage):
    sb = lambda name, shape, dt=F32: ctx.enter_context(nc.sbuf_tensor(f"{stage}_{name}", shape, dt))
    T = T_SAMPLE
    m.land = [sb(f"land{n}", [P, T]) for n in range(3)]
    m.w_raw = sb("w_raw", [P, 3, HALF, P])
    m.dist = sb("dist", [P, 2 * T - P])
    m.squares = sb("squares", [P, BLK])
    m.q_hi, m.q_lo, m.k_both = ([sb(f"{name}{n}", [P, T], F32R) for n in range(2)] for name in ("q_hi", "q_lo", "k_both"))


def normalise(nc, g, T, x, g_mix, ident, minus_half, banks, mem):
    NT = T // P
    with ExitStack() as c:
        sem = c.enter_context(semaphores(nc, f"n{g}"))
        SLOTS_X = 4
        x_in = [sem(f"x_in{s}") for s in range(SLOTS_X)]
        g_in, squared, powed, scaled, summed = sem("g_in"), sem("squared"), sem("powed"), sem("scaled"), sem("summed")
        turned, hi_done, lo_done = sem("turned"), sem("hi_done"), sem("lo_done")
        xt = mem.land[0:SLOTS_X]
        h = [mem.q[0], mem.q[1]]
        junk = mem.k[0]
        g_row = mem.k[1]
        ss, ms, rstd = mem.small[:, 0, :], mem.small[:, 1, :], mem.small[:, 2, :]
        with nc.Block() as block:

            @block.sync
            def _(sp):
                for t in range(NT):
                    if t >= SLOTS_X:
                        sp.wait_ge(scaled, t - SLOTS_X + 1)
                    sp.dma_start(xt[t % SLOTS_X][:], x[t * P:(t + 1) * P, :]).then_inc(x_in[t % SLOTS_X], 16)
                    if t == 1:
                        sp.dma_start(g_row[:], g_mix[0].partition_broadcast(P)).then_inc(g_in, 16)

            @block.scalar
            def _(act):
                def square(t):
                    act.wait_ge(x_in[t % SLOTS_X], 16 * (t // SLOTS_X + 1))
                    if t:
                        act.wait_ge(squared, t)
                    act.activation(junk[:], xt[t % SLOTS_X][:], ACT.Square, accum_out=ss[:, t:t + 1]).then_inc(squared, 1)

                square(0)
                square(1)
                for t in range(NT + 1):
                    if t + 2 < NT:
                        square(t + 2)
                    if t:
                        for b in range(2):
                            act.wait_ge(turned, 2 * (t - 1) + b + 1)
                            act.copy(mem.hT_hi[:, 4 * b:4 * b + 4, (t - 1) * P:t * P],
                                     banks[2 * ((t - 1) % 2) + b][:].rearrange("p (n c) -> p n c", c=P)
                                     ).then_inc(hi_done, 1)

            @block.gpsimd
            def _(pool):
                for t in range(NT):
                    pool.wait_ge(summed, t + 1)
                    pool.tensor_tensor(rstd[:, t:t + 1], ms[:, t:t + 1], minus_half[:, 0:1],
                                       ALU.pow).then_inc(powed, 1)

            @block.vector
            def _(dve):
                def mean(t):
                    dve.wait_ge(squared, t + 1)
                    dve.tensor_scalar(ms[:, t:t + 1], ss[:, t:t + 1], 1.0 / D, EPS, ALU.mult,
                                      ALU.add).then_inc(summed, 1)

                mean(0)
                mean(1)
                dve.wait_ge(g_in, 16)
                for t in range(NT + 1):
                    if t < NT:
                        if t + 2 < NT:
                            mean(t + 2)
                        dve.wait_ge(powed, t + 1)
                        if t >= 2:
                            dve.wait_ge(turned, 2 * (t - 1))
                        dve.scalar_tensor_tensor(h[t % 2][:], xt[t % SLOTS_X][:], rstd[:, t:t + 1], g_row[:],
                                                 ALU.mult, ALU.mult).then_inc(scaled, 1)
                    if t:
                        for b in range(2):
                            dve.wait_ge(hi_done, 2 * (t - 1) + b + 1)
                            part = (slice(None), slice(4 * b, 4 * b + 4), slice((t - 1) * P, t * P))
                            dve.tensor_tensor(mem.hT_lo[part],
                                              banks[2 * ((t - 1) % 2) + b][:].rearrange("p (n c) -> p n c", c=P),
                                              mem.hT_hi[part].bitcast(F32), ALU.subtract).then_inc(lo_done, 1)

            @block.tensor
            def _(pe):
                for t in range(NT):
                    pe.wait_ge(scaled, t + 1)
                    for b in range(2):
                        if t >= 2:
                            pe.wait_ge(lo_done, 2 * (t - 2) + b + 1)
                        for n in range(4):
                            mm = pe.transpose(banks[2 * (t % 2) + b][:, n * P:(n + 1) * P],
                                              h[t % 2][:, (4 * b + n) * P:(4 * b + n + 1) * P], ident[:])
                        mm.then_inc(turned, 1)


class Projection:

    def __init__(self, sem, T, cols, ring, by_dve, banks, w_in, mem):
        self.cols, self.ring, self.mem, self.banks = cols, ring, mem, banks
        self.w = w_in.rearrange("(n p) c -> p n c", p=P)
        self.NB = T // BLK
        self.units = 2 * len(cols)
        self.by_dve = by_dve
        self.raw_in = [Signal(sem(f"w_in{s}"), 16 * (self.units // ring)) for s in range(ring)]
        self.hi = Signal(sem("w_hi"), self.units)
        self.lo = Signal(sem("w_lo"), self.units)
        self.summed = Signal(sem("summed"), self.units * self.NB)
        self.land_act = Signal(sem("land_act"), len(cols) * self.NB)
        self.land_dve = Signal(sem("land_dve"), max(1, len(by_dve) * self.NB))
        self.uses = []
        for k in range(2):
            uses = []
            for t in range(len(cols)):
                for b in range(self.NB):
                    if self.bank_of(t, b) == k:
                        if t in by_dve:
                            uses.append(((t, b), self.land_dve, by_dve.index(t) * self.NB + b))
                        else:
                            uses.append(((t, b), self.land_act, t * self.NB + b))
            self.uses.append(Uses(uses))

    def bank_of(self, tile, b):
        return b if self.NB == 2 else tile % 2

    def load(self, sp, j, column, u):
        part = self.w[:, (u % 2) * HALF:(u % 2 + 1) * HALF, self.cols[u // 2]:self.cols[u // 2] + BLK]
        src = part[:, :, 0:P] if column is None else part[:, :, P:][:, :, bass.ds(column, P)]
        sp.wait_ge(self.lo.sem, self.lo.at(j, u - self.ring))
        sp.dma_start(self.mem.w_raw[:, u % self.ring, :, :], src).then_inc(self.raw_in[u % self.ring].sem, 16)

    def split_hi(self, act, j, u):
        arrived = self.raw_in[u % self.ring]
        act.wait_ge(arrived.sem, arrived.at(j, 16 * (u // self.ring) + 15))
        act.wait_ge(self.summed.sem, self.summed.at(j, self.NB * (u - 1) - 1))
        act.copy(self.mem.w_hi[:, u % 2, :, :], self.mem.w_raw[:, u % self.ring, :, :]).then_inc(self.hi.sem, 1)

    def split_lo(self, dve, j, u):
        dve.wait_ge(self.hi.sem, self.hi.at(j, u))
        dve.tensor_tensor(self.mem.w_lo[:, u % 2, :, :], self.mem.w_raw[:, u % self.ring, :, :],
                          self.mem.w_hi[:, u % 2, :, :].bitcast(F32), ALU.subtract).then_inc(self.lo.sem, 1)

    def multiply(self, pe, j, u, b, part):
        tile, half = divmod(u, 2)
        mem = self.mem
        if b == 0 and part == 0:
            pe.wait_ge(self.lo.sem, self.lo.at(j, u))
        out = self.banks[self.bank_of(tile, b)]
        if half == 0 and part == 0:
            pe.wait_ge(*self.uses[self.bank_of(tile, b)].before(j, (tile, b)))
        for n in range(part * HALF // CUTS, (part + 1) * HALF // CUTS):
            k = half * HALF + n
            hi, lo = mem.hT_hi[:, k, b * BLK:(b + 1) * BLK], mem.hT_lo[:, k, b * BLK:(b + 1) * BLK]
            pe.matmul(out[:], mem.w_hi[:, u % 2, n, :], hi, start=(k == 0), stop=False)
            pe.matmul(out[:], mem.w_hi[:, u % 2, n, :], lo, start=False, stop=False)
            mm = pe.matmul(out[:], mem.w_lo[:, u % 2, n, :], hi, start=False, stop=(k == DT - 1))
        if part == CUTS - 1:
            mm.then_inc(self.summed.sem, 1)

    def piece(self, n):
        u, b, part = n // (CUTS * self.NB), n // CUTS % self.NB, n % CUTS
        steps = [("unit", u, b, part)]
        if b == 0 and part == 0 and u + 1 < self.units:
            steps.insert(0, ("split", u + 1))
        if b == self.NB - 1 and part == CUTS - 1 and u % 2:
            steps.append(("land", u // 2))
        return steps


def beside(slots, proj, lead=0):
    pieces = CUTS * proj.units * proj.NB
    out, done, passed = [("split", 0)], 0, 0
    counted = lambda step: step[0] not in ("squares", "mean")
    total = sum(map(counted, slots))
    for step in slots:
        out.append(step)
        passed += counted(step)
        upto = lead + (pieces - lead) * passed // total
        for n in range(done, upto):
            out += proj.piece(n)
        done = upto
    return out


def beside_at(slots, proj):
    out = [("split", 0)]
    for step in slots:
        if step[0] == "pieces":
            for n in range(CUTS * step[1], CUTS * (step[1] + 1)):
                out += proj.piece(n)
        else:
            out.append(step)
    return out


def with_choices(steps, kind, numbers):
    numbers = list(numbers)
    each = max(1, len(numbers) // sum(step[0] == kind for step in steps))
    out = []
    for step in steps:
        out.append(step)
        if step[0] == kind:
            out += [("choose", n) for n in numbers[:each]]
            numbers = numbers[each:]
    return out


def run_heads(eng, body, first, both, last):
    for step in first:
        body(step, None, 0)
    with eng.Fori(0, HEADS - 1) as i:
        for step in both:
            body(step, i, i + 1)
    for step in last:
        body(step, HEADS - 1, None)


def hgrn(nc, g, T, w_in, masks_in, consts, banks, mem, chosen):
    NT, NB = T // P, T // BLK
    ident, slope_cols, lb, one_minus_lb, neg_lam, att_g, hg_g, carried, minus_half = consts
    with ExitStack() as c:
        sem = c.enter_context(semaphores(nc, f"h{g}"))
        X, FAR, TURN = banks[0:4], banks[4], banks[5]
        V, Q, FF_, FB, G = range(5)
        proj = Projection(sem, T, [COL_HI, COL_HQ, COL_HFF, COL_HFB, COL_HG], 5, [Q, G], banks[6:8], w_in, mem)
        mask_in = sem("mask_in")
        v_turned = Signal(sem("v_turned"), NB)
        level_read = [Signal(sem(f"level_{d}"), 8 * NB) for d in "fb"]
        k_turned = Signal(sem("k_turned"), 2 * NB)
        added = Signal(sem("added"), 2 * NB)
        o_summed = Signal(sem("o_summed"), NB)
        o_turned = Signal(sem("o_turned"), NB)
        v_rows = Signal(sem("v_rows"), NB)
        far_placed = Signal(sem("far_placed"), NB)
        k_rows = Signal(sem("k_rows"), 2 * NB)
        squared = Signal(sem("squared"), NB)
        q_taken = Signal(sem("q_taken"), 2)
        gates = Signal(sem("gates"), 2)
        updated = [Signal(sem(f"updated_{d}"), 8 * NB) for d in "fb"]
        masked = Signal(sem("masked"), 4 * NB)
        summed_up = Signal(sem("summed_up"), 4 * NB)
        state = [Signal(sem(f"state_{d}"), NT - 1) for d in "fb"]
        mean = Signal(sem("mean"), NB)
        normed = Signal(sem("normed"), NB)
        mixed = Signal(sem("mixed"), NB)
        k_made = Signal(sem("k_made"), 2)
        gate_taken = Signal(sem("gate_taken"), 1)
        placed = Signal(sem("placed"), 4 * NB)
        powed = Signal(sem("powed"), NB)

        kt_bank = lambda d, b: (2 * d + b) % 4
        ds_bank = lambda d, b: (2 * d + b + 1) % 4
        slots = [("start",)] + [("v_rows", b) for b in range(NB)]
        for b in range(NB):
            slots += [("level", b, k) for k in range(8)] + [("diag", b)]
        for d in range(2):
            slots += [("k_rows", d, b) for b in range(NB)]
            slots += [("state", d, b) for b in (range(NB) if d == 0 else reversed(range(NB)))]
        slots += [("o", 0), ("squares", 0), ("mean", 0)]
        if NB == 2:
            slots += [("o", 1), ("norm", 0), ("squares", 1), ("mean", 1), ("mix", 0)]
        slots += [("norm", NB - 1), ("mix", NB - 1)]
        first = beside([("none",)], proj)
        if g == 1:
            first = with_choices(first, "split", range(CHOICES_BEFORE["attention"][0]))
        stages = first, beside(slots, proj, NB), slots
        in_order = [s for s in slots if s[0] == "state"]
        nth = lambda step: in_order.index(step)
        first_state = lambda b, n, d: (b * BC + n == 0) if d == 0 else (b * BC + n == NT - 1)

        x_uses = []
        for s in range(4):
            uses = []
            for step in slots:
                if step[0] == "level" and step[2] == 0:
                    uses.append((step, masked, BC * step[1] + s))
                if step[0] == "k_rows" and kt_bank(*step[1:]) == s:
                    uses.append((step, k_rows, NB * step[1] + step[2]))
                if step[0] == "state" and ds_bank(*step[1:]) == s:
                    d, b = step[1:]
                    done = min((b + 1) * BC, NT - 1) if d == 0 else min((NB - b) * BC, NT - 1)
                    uses.append((step, state[d], done - 1))
            x_uses.append(Uses(uses))
        far_uses = Uses([(("level", b, 6), far_placed, b) for b in range(NB)] + [(("o", 0), normed, 0)])
        if NB == 2:
            x_uses[0].uses.append((("o", 1), normed, 1))
        o_bank = lambda b: FAR if b == 0 else X[0]
        o_uses = lambda b: far_uses if b == 0 else x_uses[0]
        turn_uses = Uses([(("v_rows", b), v_rows, b) for b in range(NB)] + [(("mix", b), mixed, b) for b in range(NB)])
        ss, ms, rstd = mem.small[:, 0, :], mem.small[:, 1, :], mem.small[:, 2, :]
        chunked = lambda bank: bank[:].rearrange("p (n c) -> p n c", c=P)

        def halves(tile, b, half):
            return tile[:, b * BLK:(b + 1) * BLK].rearrange("p (n a l) -> p n a l", a=2, l=half)

        def products(d, b, k):
            if k == 0:
                return mem.f1[d][:, b * BLK:(b + 1) * BLK]
            if k == 7:
                return mem.fend[d][:, b * BC:(b + 1) * BC]
            at = BLK - (BLK >> (k - 1))
            return mem.fup[d][:, at:at + (BLK >> k)]

        with nc.Block() as block:

            @block.sync
            def _(sp):
                start_signals(sp, proj.raw_in)
                for u in range(proj.units):
                    if u == proj.ring:
                        sp.dma_start(mem.masks[:], masks_in).then_inc(mask_in, 16)
                    proj.load(sp, 0, None, u)
                with sp.Fori(0, HEADS - 1) as i:
                    column = sp.snap(i * P)
                    for u in range(proj.units):
                        proj.load(sp, i + 1, column, u)

            @block.tensor
            def _(pe):
                start_signals(pe, [proj.summed, v_turned, *level_read, k_turned, added, o_summed, o_turned])

                def body(step, i, j):
                    kind = step[0]
                    if kind == "unit":
                        proj.multiply(pe, j, *step[1:])
                    elif kind == "v_rows":
                        b = step[1]
                        pe.wait_ge(proj.land_act.sem, proj.land_act.at(i, NB * V + b))
                        pe.wait_ge(*turn_uses.before(i, step))
                        for n in range(BC):
                            at = b * BLK + n * P
                            mm = pe.transpose(TURN[:, n * P:(n + 1) * P], mem.land[V][:, at:at + P], ident[:])
                        mm.then_inc(v_turned.sem, 1)
                    elif kind == "level":
                        b, k = step[1:]
                        if k == 6:
                            pe.wait_ge(*far_uses.before(i, step))
                        for d in range(2):
                            if k == 0:
                                pe.wait_ge(q_taken.sem, q_taken.at(i, d))
                                pe.wait_ge(k_made.sem, k_made.at(i, d))
                            else:
                                pe.wait_ge(updated[d].sem, updated[d].at(i, 8 * b + k - 1))
                            q, kk = mem.q[d], mem.k[d]
                            for n in range(BC):
                                at = b * BLK + n * P
                                if k == 0 and d == 0:
                                    pe.wait_ge(*x_uses[n].before(i, step))
                                if k < 6:
                                    for z in range(0, P, 32):
                                        mm = pe.matmul(X[n][z:z + 32, (6 * d + k) * 32:(6 * d + k + 1) * 32],
                                                       kk[:, at + z:at + z + 32], q[:, at + z:at + z + 32],
                                                       start=True, stop=True, tile_position=(0, z))
                                elif k == 6:
                                    for z in range(0, P, 64):
                                        s, t = z + 32 * d, z + 32 * (1 - d)
                                        mm = pe.matmul(FAR[s:s + 32, n * 96:n * 96 + 32], kk[:, at + s:at + s + 32],
                                                       q[:, at + t:at + t + 32], start=True, stop=True,
                                                       tile_position=(0, s))
                                else:
                                    s, t = 64 * d, 64 * (1 - d)
                                    mm = pe.matmul(FAR[s:s + 64, n * 96 + 32:n * 96 + 96], kk[:, at + s:at + s + 64],
                                                   q[:, at + t:at + t + 64], start=True, stop=True,
                                                   tile_position=(0, s))
                            mm.then_inc(level_read[d].sem, 1)
                    elif kind == "k_rows":
                        d, b = step[1:]
                        bank, uses = X[kt_bank(d, b)], x_uses[kt_bank(d, b)]
                        pe.wait_ge(updated[d].sem, updated[d].at(i, 8 * b + 7))
                        pe.wait_ge(*uses.before(i, step))
                        for n in range(BC):
                            at = b * BLK + n * P
                            mm = pe.transpose(bank[:, n * P:(n + 1) * P], mem.k[d][:, at:at + P], ident[:])
                        mm.then_inc(k_turned.sem, 1)
                    elif kind == "state":
                        d, b = step[1:]
                        bank, uses = X[ds_bank(d, b)], x_uses[ds_bank(d, b)]
                        pe.wait_ge(k_rows.sem, k_rows.at(i, NB * d + b))
                        pe.wait_ge(v_rows.sem, v_rows.at(i, b))
                        pe.wait_ge(*uses.before(i, step))
                        for n in range(BC):
                            mm = pe.matmul(bank[:, n * P:(n + 1) * P], mem.k_rows[:, b * BC + n, :],
                                           mem.v[:, b * BC + n, :], start=True, stop=True)
                        mm.then_inc(added.sem, 1)
                    elif kind == "o":
                        b = step[1]
                        pe.wait_ge(placed.sem, placed.at(i, 4 * b + 3))
                        for d in range(2):
                            pe.wait_ge(state[d].sem, state[d].last(i))
                        if b == 0:
                            pe.wait_ge(far_placed.sem, far_placed.last(i))
                        else:
                            pe.wait_ge(*x_uses[0].before(i, step))
                        for n in range(BC):
                            w = b * BC + n
                            parts = [(mem.at[:, w, :], mem.v[:, w, :])]
                            if w > 0:
                                parts.append((mem.q[0][:, w * P:(w + 1) * P], mem.state[0][:, w, :]))
                            if w < NT - 1:
                                parts.append((mem.q[1][:, w * P:(w + 1) * P], mem.state[1][:, w, :]))
                            for m, (a, r) in enumerate(parts):
                                mm = pe.matmul(o_bank(b)[:, n * P:(n + 1) * P], a, r, start=(m == 0),
                                               stop=(m == len(parts) - 1))
                        mm.then_inc(o_summed.sem, 1)
                    elif kind == "mix":
                        b = step[1]
                        pe.wait_ge(normed.sem, normed.at(i, b))
                        pe.wait_ge(*turn_uses.before(i, step))
                        for n in range(BC):
                            mm = pe.transpose(TURN[:, n * P:(n + 1) * P], mem.normed[:, n, :], ident[:])
                        mm.then_inc(o_turned.sem, 1)

                run_heads(pe, body, *stages)

            @block.scalar
            def _(act):
                start_signals(act, [proj.hi, proj.land_act, q_taken, v_rows, far_placed, k_rows, squared])
                taken = {V: v_turned, Q: q_taken, FF_: gates, FB: gates, G: gate_taken}

                def body(step, i, j):
                    kind = step[0]
                    if kind == "split":
                        proj.split_hi(act, j, step[1])
                    elif kind == "land":
                        n = step[1]
                        act.wait_ge(taken[n].sem, taken[n].last(j - 1))
                        for b in range(NB):
                            act.wait_ge(proj.summed.sem, proj.summed.at(j, (2 * n + 1) * NB + b))
                            act.activation(mem.land[n][:, b * BLK:(b + 1) * BLK], proj.banks[proj.bank_of(n, b)],
                                           ACT.Copy if n == V else ACT.Sigmoid).then_inc(proj.land_act.sem, 1)
                    elif kind == "start":
                        act.wait_ge(o_summed.sem, o_summed.last(i - 1))
                        act.wait_ge(proj.land_dve.sem, proj.land_dve.at(i, NB - 1))
                        for d in range(2):
                            act.copy(mem.q[d][:, 0:T], mem.land[Q][:, 0:T]).then_inc(q_taken.sem, 1)
                    elif kind == "v_rows":
                        b = step[1]
                        act.wait_ge(v_turned.sem, v_turned.at(i, b))
                        act.wait_ge(o_summed.sem, o_summed.last(i - 1))
                        act.copy(mem.v[:, b * BC:(b + 1) * BC, :], chunked(TURN)).then_inc(v_rows.sem, 1)
                    elif kind == "diag":
                        b = step[1]
                        act.wait_ge(o_summed.sem, o_summed.last(i - 1))
                        for d in range(2):
                            act.wait_ge(level_read[d].sem, level_read[d].at(i, 8 * b + 7))
                        far = FAR[:, 0:BC * 96].rearrange("p (n c) -> p n c", c=96)
                        at = mem.at[:, b * BC:(b + 1) * BC, :]
                        for z in range(0, P, 32):
                            t = z ^ 32
                            act.copy(at[z:z + 32, :, t:t + 32], far[z:z + 32, :, 0:32])
                        act.copy(at[0:64, :, 64:128], far[0:64, :, 32:96])
                        act.copy(at[64:128, :, 0:64], far[64:128, :, 32:96]).then_inc(far_placed.sem, 1)
                    elif kind == "k_rows":
                        d, b = step[1:]
                        act.wait_ge(k_turned.sem, k_turned.at(i, NB * d + b))
                        act.wait_ge(added.sem, added.at(i, NB * d - 1))
                        act.copy(mem.k_rows[:, b * BC:(b + 1) * BC, :], chunked(X[kt_bank(d, b)])).then_inc(k_rows.sem, 1)
                    elif kind == "squares":
                        b = step[1]
                        act.wait_ge(o_summed.sem, o_summed.at(i, b))
                        act.wait_ge(mean.sem, mean.at(i, b - NB))
                        act.wait_ge(squared.sem, squared.at(i, b - NB))
                        for n in range(BC):
                            sq = act.activation(mem.fup[b][:, n * P:(n + 1) * P], o_bank(b)[:, n * P:(n + 1) * P], ACT.Square,
                                                accum_out=ss[:, BC * b + n:BC * b + n + 1])
                        sq.then_inc(squared.sem, 1)

                run_heads(act, body, *stages)

            @block.vector
            def _(dve):
                start_signals(dve, [proj.lo, proj.land_dve, gates, *updated, masked, summed_up, *state, mean,
                                    normed, mixed])

                def level(d, b, k, i):
                    if k == 0:
                        q = mem.q[d][:, b * BLK:(b + 1) * BLK]
                        dve.tensor_tensor(q, q, products(d, b, 0), ALU.mult).then_inc(updated[d].sem, 1)
                        return
                    half = 1 << (k - 1)
                    n = BLK // (2 * half)
                    q, kk = halves(mem.q[d], b, half), halves(mem.k[d], b, half)
                    f = products(d, b, k - 1).rearrange("p (n a) -> p n a", a=2)
                    late, early = (1, 0) if d == 0 else (0, 1)
                    dve.tensor_tensor(products(d, b, k), f[:, :, 0], f[:, :, 1], ALU.mult)
                    dve.tensor_tensor(q[:, :, late, :], q[:, :, late, :],
                                      f[:, :, early:early + 1].to_broadcast([P, n, half]), ALU.mult)
                    dve.tensor_tensor(kk[:, :, early, :], kk[:, :, early, :],
                                      f[:, :, late:late + 1].to_broadcast([P, n, half]),
                                      ALU.mult).then_inc(updated[d].sem, 1)

                def body(step, i, j):
                    kind = step[0]
                    if kind == "choose":
                        chosen.step(dve, step[1])
                    elif kind == "split":
                        proj.split_lo(dve, j, step[1])
                    elif kind == "land" and step[1] in (Q, G):
                        n = step[1]
                        for b in range(NB):
                            dve.wait_ge(proj.land_act.sem, proj.land_act.at(j, NB * n + b))
                            part = mem.land[n][:, b * BLK:(b + 1) * BLK]
                            dve.tensor_tensor(part, proj.banks[proj.bank_of(n, b)][:], part,
                                              ALU.mult).then_inc(proj.land_dve.sem, 1)
                    elif kind == "start":
                        dve.wait_ge(mask_in, 16)
                        for d, n in enumerate((FF_, FB)):
                            dve.wait_ge(proj.land_act.sem, proj.land_act.at(i, NB * n + NB - 1))
                            dve.wait_ge(k_made.sem, k_made.last(i - 1))
                            dve.tensor_scalar(mem.f1[d][:, 0:T], mem.land[n][:, 0:T],
                                              one_minus_lb[:, bass.ds(i + d * HEADS, 1)],
                                              lb[:, bass.ds(i + d * HEADS, 1)], ALU.mult,
                                              ALU.add).then_inc(gates.sem, 1)
                    elif kind == "level":
                        b, k = step[1:]
                        for d in range(2):
                            dve.wait_ge(level_read[d].sem, level_read[d].at(i, 8 * b + k))
                            if k == 0:
                                dve.wait_ge(gates.sem, gates.at(i, d))
                            else:
                                dve.wait_ge(updated[d].sem, updated[d].at(i, 8 * b + k - 1))
                            level(d, b, k, i)
                    elif kind == "diag":
                        b = step[1]
                        for n in range(BC):
                            e = BC * b + n
                            dve.wait_ge(summed_up.sem, summed_up.at(i, e - 2))
                            dve.tensor_tensor(mem.masked[:, n % 2, :, :], X[n][:, 0:12 * 32].rearrange("p (k t) -> p k t", t=32),
                                              mem.masks[:], ALU.mult).then_inc(masked.sem, 1)
                            dve.wait_ge(masked.sem, masked.at(i, e))
                            if n == 0:
                                dve.wait_ge(placed.sem, placed.at(i, 4 * b - 1))
                            dve.tensor_reduce(mem.diag[:, n, :], mem.masked[:, n % 2, :, :].rearrange("p k t -> p t k"),
                                              AX_X, ALU.add).then_inc(summed_up.sem, 1)
                    elif kind == "state":
                        d, b = step[1:]
                        dve.wait_ge(added.sem, added.at(i, nth(step)))
                        dve.wait_ge(o_summed.sem, o_summed.last(i - 1))
                        add = X[ds_bank(d, b)]
                        for n in (range(BC) if d == 0 else reversed(range(BC))):
                            w = b * BC + n
                            event, to = (w, w + 1) if d == 0 else (NT - 1 - w, w - 1)
                            if event == NT - 1:
                                continue
                            if event == 0:
                                dve.tensor_copy(mem.state[d][:, to, :], add[:, n * P:(n + 1) * P]).then_inc(state[d].sem, 1)
                                continue
                            dve.wait_ge(state[d].sem, state[d].at(i, event - 1))
                            dve.scalar_tensor_tensor(mem.state[d][:, to, :], mem.state[d][:, w, :],
                                                     mem.fend[d][:, w:w + 1], add[:, n * P:(n + 1) * P],
                                                     ALU.mult, ALU.add).then_inc(state[d].sem, 1)
                    elif kind == "mean":
                        b = step[1]
                        cols = slice(BC * b, BC * (b + 1))
                        dve.wait_ge(squared.sem, squared.at(i, b))
                        dve.wait_ge(powed.sem, powed.at(i, b - NB))
                        dve.tensor_scalar(ms[:, cols], ss[:, cols], 1.0 / P, EPS, ALU.mult, ALU.add).then_inc(mean.sem, 1)
                    elif kind == "norm":
                        b = step[1]
                        dve.wait_ge(powed.sem, powed.at(i, b))
                        dve.wait_ge(o_turned.sem, o_turned.at(i, b - 1))
                        dve.tensor_tensor(mem.normed[:], chunked(o_bank(b)),
                                          rstd[:, BC * b:BC * (b + 1)].unsqueeze(2).to_broadcast([P, BC, P]),
                                          ALU.mult).then_inc(normed.sem, 1)
                    elif kind == "mix":
                        b = step[1]
                        dve.wait_ge(o_turned.sem, o_turned.at(i, b))
                        dve.wait_ge(gate_taken.sem, gate_taken.at(i, 0))
                        out = mem.mixT[:, bass.ds(i + HEADS, 1), b * BLK:(b + 1) * BLK]
                        dve.scalar_tensor_tensor(out, TURN[:].unsqueeze(1), hg_g[:, 0:1],
                                                 mem.gate[:, b * BLK:(b + 1) * BLK].unsqueeze(1),
                                                 ALU.mult, ALU.mult).then_inc(mixed.sem, 1)

                run_heads(dve, body, *stages)

            @block.gpsimd
            def _(pool):
                start_signals(pool, [k_made, gate_taken, placed, powed])
                carry = Carrier(pool, carried[1], minus_half)

                def body(step, i, j):
                    kind = step[0]
                    if kind == "start":
                        pool.wait_ge(o_summed.sem, o_summed.last(i - 1))
                        for d in range(2):
                            pool.wait_ge(gates.sem, gates.at(i, d))
                            carry()
                            pool.tensor_scalar(mem.k[d][:, 0:T], mem.f1[d][:, 0:T], -1.0, 1.0, ALU.mult,
                                               ALU.add).then_inc(k_made.sem, 1)
                        pool.wait_ge(proj.land_dve.sem, proj.land_dve.at(i, 2 * NB - 1))
                        pool.wait_ge(mixed.sem, mixed.last(i - 1))
                        carry()
                        pool.tensor_copy(mem.gate[:, 0:T], mem.land[G][:, 0:T]).then_inc(gate_taken.sem, 1)
                    elif kind == "diag":
                        b = step[1]
                        pool.wait_ge(summed_up.sem, summed_up.at(i, BC * b + BC - 1))
                        pool.wait_ge(gate_taken.sem, gate_taken.at(i, 0))
                        for n, z in enumerate(range(0, P, 32)):
                            pool.wait_ge(placed.sem, placed.at(i, 4 * b + n - 1))
                            carry(slice(z, z + 32))
                            pool.tensor_copy(mem.at[z:z + 32, b * BC:(b + 1) * BC, z:z + 32],
                                             mem.diag[z:z + 32, :, :]).then_inc(placed.sem, 1)
                    elif kind == "mean":
                        b = step[1]
                        pool.wait_ge(placed.sem, placed.last(i))
                        pool.wait_ge(mean.sem, mean.at(i, b))
                        pool.wait_ge(normed.sem, normed.at(i, b - NB))
                        cols = slice(BC * b, BC * (b + 1))
                        pool.tensor_tensor(rstd[:, cols], ms[:, cols], minus_half[:, 0:BC], ALU.pow).then_inc(powed.sem, 1)

                run_heads(pool, body, *stages)


def attention(nc, g, T, w_in, dist_in, consts, banks, mem, chosen):
    NT, NB = T // P, T // BLK
    ident, slope_cols, lb, one_minus_lb, neg_lam, att_g, hg_g, carried, minus_half = consts
    with ExitStack() as c:
        sem = c.enter_context(semaphores(nc, f"a{g}"))
        TURN, OUT = banks[4], banks[5]
        Q, K, V = range(3)
        proj = Projection(sem, T, [COL_AQ, COL_AK, COL_AV], 3, [], banks[6:8], w_in, mem)
        dist_ready = sem("dist_ready")
        v_turned = Signal(sem("v_turned"), NB)
        scored = Signal(sem("scored"), 2 * NT)
        w_turned = Signal(sem("w_turned"), NT * NB)
        summed = Signal(sem("o_summed"), NT)
        o_turned = Signal(sem("o_turned"), NB)
        v_rows = Signal(sem("v_rows"), NB)
        k_first, q_first = Signal(sem("k_first"), 2), Signal(sem("q_first"), 2)
        exped = Signal(sem("exped"), 2 * NT)
        w_rows = Signal(sem("w_rows"), NT * NB)
        squared = Signal(sem("squared"), NB)
        slopes = Signal(sem("slopes"), 1)
        biased = Signal(sem("biased"), 2 * NT)
        ratio = Signal(sem("ratio"), 3 * NT)
        weighed = Signal(sem("weighed"), NT)
        scales = Signal(sem("scales"), 4 * NB)
        rescaled = Signal(sem("rescaled"), NB)
        normed = Signal(sem("normed"), NB)
        mixed = Signal(sem("mixed"), NB)
        taken = Signal(sem("taken"), 2)
        powed = Signal(sem("powed"), NB)

        last = proj.units * NB
        slots = [(kind, 0, m) for m in range(2) for kind in ("scores", "exp")]
        slots += [("pieces", 0)] + [("v_rows", b) for b in range(NB)]
        for t in range(NT + 1):
            if t == NT:
                slots.append(("pieces", NT - 1 + NB))
            if t:
                slots.append(("turn", t - 1, 0))
            if t + 1 < NT:
                slots.append(("scores", t + 1, 0))
            if t and NB == 2:
                slots.append(("turn", t - 1, 1))
            if t + 1 < NT:
                slots += [("exp", t + 1, 0), ("scores", t + 1, 1), ("exp", t + 1, 1)]
            if t < NT:
                slots.append(("weigh", t))
            if t == NT - 1:
                slots.append(("take",))
            if t < NT - 2 + NB:
                slots.append(("pieces", t + 1))
            if t:
                slots.append(("out", t - 1))
                if t > BC and t % BC == 1:
                    slots.append(("mix", t // BC - 1))
                if t % BC == 0:
                    slots += [("squares", t // BC - 1), ("mean", t // BC - 1), ("norm", t // BC - 1)]
        slots += [("pieces", n) for n in range(NT + NB, last)] + [("mix", NB - 1)]
        alone = [s for s in slots if s[0] not in ("pieces", "take")]
        first = [("pieces", n) for n in range(last)]
        first.insert(4 * NB, ("take",))
        first = beside_at(first, proj)
        if g == 1:
            first = with_choices(first, "split", range(*CHOICES_BEFORE["attention"]))
            alone = with_choices(alone, "weigh", range(CHOICES_BEFORE["attention"][1], CHOICES_BEFORE["out"]))
        stages = first, beside_at(slots, proj), alone

        def score_banks(t, j):
            return banks[2 * j:2 * j + 2] if NB == 2 else [banks[2 * j + t % 2]]

        turn_uses = []
        for step in slots:
            if step[0] == "v_rows":
                turn_uses.append((step, v_rows, step[1]))
            if step[0] == "turn":
                turn_uses.append((step, w_rows, NB * step[1] + step[2]))
            if step[0] == "mix":
                turn_uses.append((step, mixed, step[1]))
        turn_uses = Uses(turn_uses)
        chunked = lambda bank: bank[:].rearrange("p (n c) -> p n c", c=P)
        small = mem.small
        row_sum, cross = small[:, 0:2, :], small[:, 2, :]
        low = small[:, 3, :]
        ss, ms, rstd, inv = small[:, 4, :], small[:, 5, :], small[:, 6, :], small[:, 7, :]
        q_hi, q_lo, k_both = mem.q_hi, mem.q_lo, mem.k_both
        rows_of = lambda m: slice(QK * m, QK * (m + 1))
        scores = [mem.k[0], mem.k[1]]
        probs = [[mem.q[0], mem.q[1]], [mem.f1[0], mem.f1[1]]]
        weights = [mem.state[0][:].rearrange("p n c -> p (n c)"), mem.state[1][:].rearrange("p n c -> p (n c)")]
        w_keys = mem.k_rows
        slope_now = small[:, 0, 15:16]

        with nc.Block() as block:

            @block.sync
            def _(sp):
                start_signals(sp, proj.raw_in)
                for u in range(proj.units):
                    if u == proj.ring:
                        sp.dma_start(mem.dist[:], dist_in).then_inc(dist_ready, 16)
                    proj.load(sp, 0, None, u)
                with sp.Fori(0, HEADS - 1) as i:
                    column = sp.snap(i * P)
                    for u in range(proj.units):
                        proj.load(sp, i + 1, column, u)

            @block.tensor
            def _(pe):
                start_signals(pe, [proj.summed, v_turned, scored, w_turned, summed, o_turned])

                def body(step, i, j):
                    kind = step[0]
                    if kind == "unit":
                        proj.multiply(pe, j, *step[1:])
                    elif kind == "v_rows":
                        b = step[1]
                        pe.wait_ge(proj.land_act.sem, proj.land_act.at(i, NB * V + b))
                        pe.wait_ge(*turn_uses.before(i, step))
                        for n in range(BC):
                            at = b * BLK + n * P
                            mm = pe.transpose(TURN[:, n * P:(n + 1) * P], mem.land[V][:, at:at + P], ident[:])
                        mm.then_inc(v_turned.sem, 1)
                    elif kind == "scores":
                        t, m = step[1:]
                        pe.wait_ge(taken.sem, taken.at(i, 1))
                        pe.wait_ge(biased.sem, biased.at(i, 2 * (t - 3 + NB) + m))
                        for b, bank in enumerate(score_banks(t, m)):
                            keys = k_both[m][:, b * BLK:(b + 1) * BLK]
                            pe.matmul(bank[:], q_hi[m][:, t * P:(t + 1) * P], keys, start=True, stop=False)
                            mm = pe.matmul(bank[:], q_lo[m][:, t * P:(t + 1) * P], keys, start=False, stop=True)
                        mm.then_inc(scored.sem, 1)
                    elif kind == "turn":
                        t, b = step[1:]
                        pe.wait_ge(weighed.sem, weighed.at(i, t))
                        pe.wait_ge(*turn_uses.before(i, step))
                        for n in range(BC):
                            at = b * BLK + n * P
                            mm = pe.transpose(TURN[:, n * P:(n + 1) * P], weights[t % 2][:, at:at + P], ident[:])
                        mm.then_inc(w_turned.sem, 1)
                    elif kind == "out":
                        t = step[1]
                        pe.wait_ge(w_rows.sem, w_rows.at(i, NB * t + NB - 1))
                        pe.wait_ge(v_rows.sem, v_rows.last(i))
                        if t % BC == 0:
                            pe.wait_ge(normed.sem, normed.at(i, t // BC - 1))
                        for n in range(NT):
                            mm = pe.matmul(OUT[:, (t % BC) * P:(t % BC + 1) * P], w_keys[:, n, :], mem.v[:, n, :],
                                           start=(n == 0), stop=(n == NT - 1))
                        mm.then_inc(summed.sem, 1)
                    elif kind == "mix":
                        b = step[1]
                        pe.wait_ge(normed.sem, normed.at(i, b))
                        pe.wait_ge(*turn_uses.before(i, step))
                        for n in range(BC):
                            mm = pe.transpose(TURN[:, n * P:(n + 1) * P], mem.normed[:, n, :], ident[:])
                        mm.then_inc(o_turned.sem, 1)

                run_heads(pe, body, *stages)

            @block.scalar
            def _(act):
                start_signals(act, [proj.hi, proj.land_act, k_first, q_first, v_rows, exped, w_rows, squared])

                def body(step, i, j):
                    kind = step[0]
                    if kind == "split":
                        proj.split_hi(act, j, step[1])
                    elif kind == "land":
                        n = step[1]
                        if n == V:
                            act.wait_ge(v_turned.sem, v_turned.last(j - 1))
                        else:
                            act.wait_ge(taken.sem, taken.last(j - 1))
                        for b in range(NB):
                            act.wait_ge(proj.summed.sem, proj.summed.at(j, (2 * n + 1) * NB + b))
                            to, of = mem.land[n][:, b * BLK:(b + 1) * BLK], proj.banks[proj.bank_of(n, b)]
                            act.copy(to, of).then_inc(proj.land_act.sem, 1)
                    elif kind == "v_rows":
                        b = step[1]
                        act.wait_ge(v_turned.sem, v_turned.at(i, b))
                        act.wait_ge(summed.sem, summed.last(i - 1))
                        act.copy(mem.v[:, b * BC:(b + 1) * BC, :], chunked(TURN)).then_inc(v_rows.sem, 1)
                    elif kind == "take":
                        act.wait_ge(proj.land_act.sem, proj.land_act.at(j, NB * K + NB - 1))
                        act.wait_ge(scored.sem, scored.last(j - 1))
                        for m in range(2):
                            act.copy(k_both[m][rows_of(m), 0:T], mem.land[K][rows_of(m), 0:T]).then_inc(k_first.sem, 1)
                        for m in range(2):
                            for half in range(2):
                                high = act.activation(q_hi[m][rows_of(half), 0:T], mem.land[Q][rows_of(m), 0:T], ACT.Copy,
                                                      scale=slope_cols[rows_of(m), 0, bass.ds(j, 1)])
                            high.then_inc(q_first.sem, 1)
                    elif kind == "exp":
                        t, m = step[1:]
                        act.wait_ge(weighed.sem, weighed.at(i, t - 2))
                        act.wait_ge(biased.sem, biased.at(i, 2 * t + m))
                        act.activation(probs[t % 2][m][:, 0:T], scores[m][:, 0:T], ACT.Exp, scale=-1.0,
                                       bias=low[:, m:m + 1], accum_out=row_sum[:, m, t % BC:t % BC + 1]
                                       ).then_inc(exped.sem, 1)
                    elif kind == "turn":
                        t, b = step[1:]
                        act.wait_ge(w_turned.sem, w_turned.at(i, NB * t + b))
                        act.wait_ge(summed.sem, summed.at(i, t - 1))
                        act.copy(w_keys[:, b * BC:(b + 1) * BC, :], chunked(TURN)).then_inc(w_rows.sem, 1)
                    elif kind == "squares":
                        b = step[1]
                        act.wait_ge(summed.sem, summed.at(i, BC * b + BC - 1))
                        act.wait_ge(scales.sem, scales.at(i, 4 * b - 1))
                        for n in range(BC):
                            sq = act.activation(mem.squares[:, n * P:(n + 1) * P], OUT[:, n * P:(n + 1) * P], ACT.Square,
                                                accum_out=ss[:, n:n + 1])
                        sq.then_inc(squared.sem, 1)

                run_heads(act, body, *stages)

            @block.vector
            def _(dve):
                carry = Carrier(dve, carried[0], minus_half)
                start_signals(dve, [proj.lo, slopes, taken, biased, ratio, weighed, scales, rescaled, normed, mixed])

                def body(step, i, j):
                    kind = step[0]
                    if kind == "choose":
                        chosen.step(dve, step[1])
                    elif kind == "split":
                        proj.split_lo(dve, j, step[1])
                    elif kind == "take":
                        dve.wait_ge(dist_ready, 16)
                        dve.wait_ge(scored.sem, scored.last(j - 1))
                        for m in range(2):
                            dve.wait_ge(k_first.sem, k_first.at(j, m))
                            made = dve.tensor_tensor(k_both[m][rows_of(1 - m), 0:T], mem.land[K][rows_of(m), 0:T],
                                                    k_both[m][rows_of(m), 0:T].bitcast(F32), ALU.subtract)
                        made.then_inc(taken.sem, 1)
                        for m in range(2):
                            dve.wait_ge(q_first.sem, q_first.at(j, m))
                            for half in range(2):
                                made = dve.scalar_tensor_tensor(q_lo[m][rows_of(half), 0:T], mem.land[Q][rows_of(m), 0:T],
                                                               slope_cols[rows_of(m), 0, bass.ds(j, 1)],
                                                               q_hi[m][rows_of(m), 0:T].bitcast(F32), ALU.mult, ALU.subtract)
                        made.then_inc(taken.sem, 1)
                        dve.tensor_copy(slope_now, slope_cols[:, 1, bass.ds(j, 1)]).then_inc(slopes.sem, 1)
                        dve.wait_ge(slopes.sem, slopes.at(j, 0))
                    elif kind == "scores":
                        t, m = step[1:]
                        dve.wait_ge(scored.sem, scored.at(i, 2 * t + m))
                        dve.wait_ge(exped.sem, exped.at(i, 2 * (t - 1) + m))
                        carry()
                        at = T_SAMPLE - P - t * P
                        psum = mem.pairs[m][:, 0:T] if NB == 2 else score_banks(t, m)[0][:]
                        dve.tensor_tensor_reduce(out=scores[m][:, 0:T], in0=psum, in1=mem.dist[:, at:at + T],
                                                 scale=slope_now, scalar=BIG, op0=ALU.add, op1=ALU.min,
                                                 accum_out=low[:, m:m + 1]).then_inc(biased.sem, 1)
                    elif kind == "weigh":
                        t = step[1]
                        dve.wait_ge(exped.sem, exped.at(i, 2 * t + 1))
                        dve.wait_ge(weighed.sem, weighed.at(i, t - 1))
                        q = t % BC
                        if t == 0:
                            dve.wait_ge(scales.sem, scales.last(i - 1))
                        dve.reciprocal(cross[:, 0:1], row_sum[:, 1, q:q + 1]).then_inc(ratio.sem, 1)
                        dve.tensor_copy(inv[:, 4 + t:5 + t], row_sum[:, 0, q:q + 1]).then_inc(ratio.sem, 1)
                        dve.wait_ge(ratio.sem, ratio.at(i, 3 * t + 1))
                        dve.tensor_scalar(cross[:, 1:2], cross[:, 0:1], row_sum[:, 0, q:q + 1], neg_lam[:, 0:1],
                                          ALU.mult, ALU.mult).then_inc(ratio.sem, 1)
                        dve.wait_ge(ratio.sem, ratio.at(i, 3 * t + 2))
                        dve.wait_ge(w_turned.sem, w_turned.at(i, NB * (t - 2) + NB - 1))
                        dve.scalar_tensor_tensor(weights[t % 2][:, 0:T], probs[t % 2][1][:, 0:T], cross[:, 1:2],
                                                 probs[t % 2][0][:, 0:T], ALU.mult, ALU.add).then_inc(weighed.sem, 1)
                    elif kind == "mean":
                        b = step[1]
                        dve.wait_ge(ratio.sem, ratio.at(i, 3 * (BC * b + BC - 1) + 2))
                        dve.reciprocal(inv[:, 0:BC], inv[:, 4 + BC * b:4 + BC * (b + 1)]).then_inc(scales.sem, 1)
                        dve.wait_ge(scales.sem, scales.at(i, 4 * b))
                        dve.wait_ge(squared.sem, squared.at(i, b))
                        dve.wait_ge(powed.sem, powed.at(i, b - 1))
                        dve.tensor_tensor(ms[:, 0:BC], ss[:, 0:BC], inv[:, 0:BC], ALU.mult).then_inc(scales.sem, 1)
                        dve.wait_ge(scales.sem, scales.at(i, 4 * b + 1))
                        dve.tensor_tensor(ms[:, 4:4 + BC], ms[:, 0:BC], inv[:, 0:BC], ALU.mult).then_inc(scales.sem, 1)
                        dve.wait_ge(scales.sem, scales.at(i, 4 * b + 2))
                        dve.tensor_scalar(ms[:, 8:8 + BC], ms[:, 4:4 + BC], 1.0 / P, EPS, ALU.mult,
                                          ALU.add).then_inc(scales.sem, 1)
                    elif kind == "norm":
                        b = step[1]
                        dve.wait_ge(powed.sem, powed.at(i, b))
                        dve.tensor_tensor(rstd[:, 4:4 + BC], rstd[:, 0:BC], inv[:, 0:BC], ALU.mult).then_inc(rescaled.sem, 1)
                        dve.wait_ge(rescaled.sem, rescaled.at(i, b))
                        dve.wait_ge(o_turned.sem, o_turned.at(i, b - 1))
                        dve.tensor_tensor(mem.normed[:], chunked(OUT),
                                          rstd[:, 4:4 + BC].unsqueeze(2).to_broadcast([P, BC, P]),
                                          ALU.mult).then_inc(normed.sem, 1)
                    elif kind == "mix":
                        b = step[1]
                        dve.wait_ge(o_turned.sem, o_turned.at(i, b))
                        out = mem.mixT[:, bass.ds(i, 1), b * BLK:(b + 1) * BLK]
                        dve.tensor_scalar(out, TURN[:].unsqueeze(1), att_g[:, 0:1], None, ALU.mult).then_inc(mixed.sem, 1)

                run_heads(dve, body, *stages)

            @block.gpsimd
            def _(pool):
                start_signals(pool, [powed])

                def body(step, i, j):
                    kind = step[0]
                    if kind == "mean":
                        b = step[1]
                        pool.wait_ge(scales.sem, scales.at(i, 4 * b + 3))
                        pool.wait_ge(normed.sem, normed.at(i, b - 1))
                        pool.tensor_tensor(rstd[:, 0:BC], ms[:, 8:8 + BC], minus_half[:, 0:BC], ALU.pow).then_inc(powed.sem, 1)

                run_heads(pool, body, *stages)


def project_out(nc, g, T, x, row, w_out, g_ffn, w_router, consts, banks, mem, aff, h2_dram, y_dram,
                chosen):
    NT = T // P
    ident, minus_half = consts[0], consts[-1]
    with ExitStack() as c:
        sem = c.enter_context(semaphores(nc, f"o{g}"))
        w_in = [sem(f"w_in{s}") for s in range(4)]
        x_in = [sem(f"x_in{s}") for s in range(2)]
        g_in, r_in = sem("g_in"), sem("r_in")
        w_hi, w_lo = sem("w_hi"), sem("w_lo")
        m_hi, m_lo, m_used = sem("m_hi"), sem("m_lo"), sem("m_used")
        added, squared, mean, powed, normed = sem("added"), sem("squared"), sem("mean"), sem("powed"), sem("normed")
        y_out, h_out = [sem(f"y_out{s}") for s in range(2)], [sem(f"h_out{s}") for s in range(2)]
        turned, h_turned, logits = sem("turned"), sem("h_turned"), sem("logits")
        highest, exped, inverse, shares, shares_turned, placed = (sem(s) for s in ("highest", "exped", "inverse", "shares", "shares_turned", "placed"))
        raw = mem.land[0:4]
        xr, x1, h2 = mem.q, mem.k, mem.f1
        g_row = mem.gate
        h2T = mem.state[0]
        router = mem.masks[:].rearrange("p a b -> p (a b)")[:, 0:DT * EXPERTS].rearrange("p (n e) -> p n e", e=EXPERTS)
        small = mem.small
        ss, ms, rstd, top, total, inv = (small[:, n, :] for n in range(6))
        e_row, a_row = small[:, 6, :], small[:, 7, :]
        rows = aff[0:16, :] if row == 0 else aff[PROMPT_ROW:PROMPT_ROW + 16, :]
        chunked = lambda bank: bank[:].rearrange("p (n c) -> p n c", c=P)
        with nc.Block() as block:

            @block.sync
            def _(sp):
                for k in range(DT):
                    if k == 4:
                        sp.dma_start(g_row[:], g_ffn[0].partition_broadcast(P)).then_inc(g_in, 16)
                        sp.dma_start(router, w_router).then_inc(r_in, 16)
                    if k >= 4:
                        sp.wait_ge(w_lo, k - 3)
                    sp.dma_start(raw[k % 4][:], w_out[0, k * P:(k + 1) * P, :]).then_inc(w_in[k % 4], 16)
                for t in range(NT + 1):
                    if t < NT:
                        if t >= 2:
                            sp.wait_ge(added, 2 * (t - 1))
                        sp.dma_start(xr[t % 2][:], x[t * P:(t + 1) * P, :]).then_inc(x_in[t % 2], 16)
                    if t:
                        at = row + (t - 1) * P
                        sp.wait_ge(added, 2 * t)
                        sp.dma_start(y_dram[at:at + P, :], x1[(t - 1) % 2][:]).then_inc(y_out[(t - 1) % 2], 16)
                        sp.wait_ge(normed, t)
                        sp.dma_start(h2_dram[at:at + P, :], h2[(t - 1) % 2][:]).then_inc(h_out[(t - 1) % 2], 16)
                for s in range(2):
                    sp.wait_ge(y_out[s], 16 * (NT // 2))
                    sp.wait_ge(h_out[s], 16 * (NT // 2))

            @block.tensor
            def _(pe):
                def transposes(t):
                    pe.wait_ge(normed, t + 1)
                    for b in range(2):
                        if t:
                            pe.wait_ge(h_turned, 2 * (t - 1) + b + 1)
                        for n in range(4):
                            at = (4 * b + n) * P
                            mm = pe.transpose(banks[4 + b][:, n * P:(n + 1) * P], h2[t % 2][:, at:at + P], ident[:])
                        mm.then_inc(turned, 1)

                def route(t):
                    if t == 0:
                        pe.wait_ge(r_in, 16)
                    pe.wait_ge(h_turned, 2 * (t + 1))
                    if t:
                        pe.wait_ge(exped, t)
                    for n in range(DT):
                        mm = pe.matmul(banks[6][:, 0:EXPERTS], h2T[:, n, :], router[:, n, :], start=(n == 0),
                                       stop=(n == DT - 1))
                    mm.then_inc(logits, 1)

                def turn_shares(t):
                    pe.wait_ge(shares, t + 1)
                    if t:
                        pe.wait_ge(placed, t)
                    pe.transpose(banks[7][0:EXPERTS, 0:P], a_row, ident[:]).then_inc(shares_turned, 1)

                for t in range(NT + 1):
                    if t < NT:
                        if t >= 2:
                            pe.wait_ge(added, 2 * (t - 1))
                        for half in range(2):
                            u = 2 * t + half
                            pe.wait_ge(m_lo, u + 1)
                            for n in range(HALF):
                                k = half * HALF + n
                                if t == 0:
                                    pe.wait_ge(w_lo, k + 1)
                                for h in range(2):
                                    out = banks[2 * (t % 2) + h][:]
                                    hi, lo = (w[:, k, h * BLK:(h + 1) * BLK] for w in (mem.hT_hi, mem.hT_lo))
                                    pe.matmul(out, mem.w_hi[:, u % 2, n, :], hi, start=(k == 0), stop=False)
                                    pe.matmul(out, mem.w_hi[:, u % 2, n, :], lo, start=False, stop=False)
                                    mm = pe.matmul(out, mem.w_lo[:, u % 2, n, :], hi, start=False, stop=(k == DT - 1))
                            mm.then_inc(m_used, 1)
                            if t and half == 0:
                                transposes(t - 1)
                        if t:
                            route(t - 1)
                    else:
                        transposes(t - 1)
                        route(t - 1)
                    if t >= 2:
                        turn_shares(t - 2)
                turn_shares(NT - 1)

            @block.scalar
            def _(act):
                def split(u):
                    if u >= 2:
                        act.wait_ge(m_used, u - 1)
                    t, half = divmod(u, 2)
                    act.copy(mem.w_hi[:, u % 2, :, :], mem.mixT[:, half * HALF:(half + 1) * HALF, t * P:(t + 1) * P]).then_inc(m_hi, 1)

                def square(t):
                    act.wait_ge(added, 2 * t + 2)
                    if t:
                        act.wait_ge(squared, t)
                    act.activation(mem.land[4][:], x1[t % 2][:], ACT.Square, accum_out=ss[:, t:t + 1]).then_inc(squared, 1)

                def take_turned(t):
                    for b in range(2):
                        act.wait_ge(turned, 2 * t + b + 1)
                        if t:
                            act.wait_ge(logits, t)
                        act.copy(h2T[:, 4 * b:4 * b + 4, :], chunked(banks[4 + b])).then_inc(h_turned, 1)

                def exps(t):
                    act.wait_ge(highest, t + 1)
                    if t:
                        act.wait_ge(shares, t)
                    act.activation(e_row, banks[6][:, 0:EXPERTS], ACT.Exp, bias=top[:, t:t + 1],
                                   accum_out=total[:, t:t + 1]).then_inc(exped, 1)

                def place(t):
                    act.wait_ge(shares_turned, t + 1)
                    act.copy(rows[:, t * P:(t + 1) * P], banks[7][0:EXPERTS, 0:P]).then_inc(placed, 1)

                split(0)
                split(1)
                for k in range(DT):
                    act.wait_ge(w_in[k % 4], 16 * (k // 4 + 1))
                    act.copy(mem.hT_hi[:, k, :], raw[k % 4][:]).then_inc(w_hi, 1)
                for t in range(NT + 1):
                    if t + 1 < NT:
                        split(2 * t + 2)
                    if t:
                        take_turned(t - 1)
                    if t + 1 < NT:
                        split(2 * t + 3)
                    if t < NT:
                        square(t)
                    if t:
                        exps(t - 1)
                    if t >= 2:
                        place(t - 2)
                place(NT - 1)

            @block.gpsimd
            def _(pool):
                for t in range(NT):
                    pool.wait_ge(mean, t + 1)
                    pool.tensor_tensor(rstd[:, t:t + 1], ms[:, t:t + 1], minus_half[:, 0:1], ALU.pow).then_inc(powed, 1)

            @block.vector
            def _(dve):
                def split(u):
                    dve.wait_ge(m_hi, u + 1)
                    t, half = divmod(u, 2)
                    dve.tensor_tensor(mem.w_lo[:, u % 2, :, :], mem.mixT[:, half * HALF:(half + 1) * HALF, t * P:(t + 1) * P],
                                      mem.w_hi[:, u % 2, :, :].bitcast(F32), ALU.subtract).then_inc(m_lo, 1)

                def rows_of(t):
                    dve.wait_ge(x_in[t % 2], 16 * (t // 2 + 1))
                    dve.wait_ge(m_used, 2 * t + 2)
                    if t >= 2:
                        dve.wait_ge(y_out[t % 2], 16 * (t // 2))
                        dve.wait_ge(squared, t - 1)
                    for h in range(2):
                        part = slice(h * BLK, (h + 1) * BLK)
                        dve.tensor_tensor(x1[t % 2][:, part], banks[2 * (t % 2) + h][:], xr[t % 2][:, part],
                                          ALU.add).then_inc(added, 1)

                def norm(t):
                    dve.wait_ge(squared, t + 1)
                    dve.tensor_scalar(ms[:, t:t + 1], ss[:, t:t + 1], 1.0 / D, EPS, ALU.mult, ALU.add).then_inc(mean, 1)
                    dve.wait_ge(powed, t + 1)
                    if t >= 2:
                        dve.wait_ge(h_out[t % 2], 16 * (t // 2))
                        dve.wait_ge(turned, 2 * (t - 1))
                    if t == 0:
                        dve.wait_ge(g_in, 16)
                    dve.scalar_tensor_tensor(h2[t % 2][:], x1[t % 2][:], rstd[:, t:t + 1], g_row[:], ALU.mult,
                                             ALU.mult).then_inc(normed, 1)

                def tail(t):
                    dve.wait_ge(logits, t + 1)
                    dve.tensor_reduce(top[:, t:t + 1], banks[6][:, 0:EXPERTS], AX_X, ALU.max, negate=True).then_inc(highest, 1)
                    dve.wait_ge(exped, t + 1)
                    dve.reciprocal(inv[:, t:t + 1], total[:, t:t + 1]).then_inc(inverse, 1)
                    dve.wait_ge(inverse, t + 1)
                    if t:
                        dve.wait_ge(shares_turned, t)
                    dve.tensor_scalar(a_row, e_row, inv[:, t:t + 1], None, ALU.mult).then_inc(shares, 1)

                split(0)
                split(1)
                for k in range(DT):
                    dve.wait_ge(w_hi, k + 1)
                    dve.tensor_tensor(mem.hT_lo[:, k, :], raw[k % 4][:], mem.hT_hi[:, k, :].bitcast(F32),
                                      ALU.subtract).then_inc(w_lo, 1)
                for t in range(NT + 1):
                    if t + 1 < NT:
                        split(2 * t + 2)
                    if t < NT:
                        rows_of(t)
                    if t + 1 < NT:
                        split(2 * t + 3)
                    if t < NT:
                        norm(t)
                    if t:
                        tail(t - 1)
                    if g == 1 and t < NT:
                        each = (CHOICES - CHOICES_BEFORE["out"]) // NT
                        for n in range(each):
                            chosen.step(dve, CHOICES_BEFORE["out"] + each * t + n)


def choose(nc, ctx, ident, banks, aff, shares, index):
    index_cols = ctx.enter_context(nc.sbuf_tensor("index_cols", [P, 2, EXPERTS], I32))
    gate_cols = ctx.enter_context(nc.sbuf_tensor("gate_cols", [P, 2, EXPERTS], F32))
    with ExitStack() as c:
        sem = c.enter_context(semaphores(nc, "c"))
        sb = lambda name, shape, dt=F32: c.enter_context(nc.sbuf_tensor(name, shape, dt))
        index_f = sb("index_f", [48, P])
        filled, found, turned, taken = sem("filled"), sem("found"), sem("turned"), sem("taken")
        prompt = slice(PROMPT_ROW, PROMPT_ROW + EXPERTS)
        rounds = Rounds(found, aff[prompt, 0:T_PROMPT], shares[prompt, :], index[prompt, :])
        steps = 3 * CAP_PROMPT // TOP
        with nc.Block() as block:

            @block.gpsimd
            def _(pool):
                pool.memset(index_f[:], 0.0).then_inc(filled, 1)

            @block.vector
            def _(dve):
                dve.wait_ge(filled, 1)
                for n in range(steps):
                    rounds.step(dve, n)
                dve.wait_ge(found, steps)
                for part in ((slice(0, EXPERTS), slice(None)), (prompt, slice(0, CAP_PROMPT))):
                    dve.tensor_copy(index_f[part], index[part]).then_inc(found, 1)
                dve.tensor_copy(shares[prompt, CAP_PROMPT:P], shares[prompt, 0:CAP_PROMPT]).then_inc(found, 1)
                dve.wait_ge(turned, 1)
                dve.tensor_scalar(index_cols[:, 0, :], banks[0][:, PROMPT_ROW:PROMPT_ROW + EXPERTS],
                                  float(T_SAMPLE), None, ALU.add).then_inc(taken, 1)
                dve.tensor_copy(index_cols[:, 1, :], banks[0][:, 0:EXPERTS]).then_inc(taken, 1)
                dve.tensor_copy(gate_cols[:, 0, :], banks[1][:, PROMPT_ROW:PROMPT_ROW + EXPERTS]).then_inc(taken, 1)
                dve.tensor_copy(gate_cols[:, 1, :], banks[1][:, 0:EXPERTS]).then_inc(taken, 1)

            @block.tensor
            def _(pe):
                pe.wait_ge(found, steps + 3)
                pe.transpose(banks[0][:, 0:48], index_f[:], ident[0:48, 0:48])
                pe.transpose(banks[1][:, 0:48], shares[:], ident[0:48, 0:48]).then_inc(turned, 1)

    return index_cols, gate_cols


def experts(nc, ctx, w_gate, w_up, w_down, ident, minus_half, psum, banks, index_cols, gate_cols, h2_dram, y_dram):
    RAW, PARTS, PAIRS, UNITS = 8, 4, EXPERTS // 2, 3 * DT
    Q = DT // 2
    with ExitStack() as c:
        sem = c.enter_context(semaphores(nc, "e"))
        sb = lambda name, shape, dt=F32: c.enter_context(nc.sbuf_tensor(name, shape, dt))
        raw = sb("raw", [P, RAW, FF])
        w_hi, w_lo = sb("we_hi", [P, PARTS, FF], F32R), sb("we_lo", [P, PARTS, FF], F32R)
        rows_p, rows_s = sb("rows_p", [CAP_PROMPT, D]), sb("rows_s", [P, D])
        x_parts = sb("x_parts", [P, DT, 2, SLOTS], F32R)
        x_hi, x_lo = (x_parts[:, :, n, :] for n in range(2))
        hid_parts = sb("hid_parts", [P, FT, 2 * SLOTS], F32R)
        hid_both, hid_lo = hid_parts[:, :, 0:2 * CAP_PROMPT], hid_parts[:, :, CAP_PROMPT:CAP_PROMPT + SLOTS]
        hid_hi = {slice(0, CAP_PROMPT): hid_parts[:, :, 0:CAP_PROMPT],
                  slice(CAP_PROMPT, SLOTS): hid_parts[:, :, CAP_PROMPT + SLOTS:]}
        sample_slots = slice(CAP_PROMPT, SLOTS)
        silu, hid = sb("silu", [P, FT, SLOTS]), sb("hid", [P, FT, SLOTS])
        low_rows = sb("low_rows", [CAP_PROMPT, D])
        result_p, result_s = sb("result_p", [CAP_PROMPT, D]), sb("result_s", [P, D])
        carried_act = sb("carried_act", [P, 1])
        carried_pool = sb("carried_pool", [P, 6])
        index_p = sb("index_p", [CAP_PROMPT, 2], I32)
        index_s = sb("index_s", [P, 2], I32)

        raw_in = [Signal(sem(f"raw_in{s}"), 2 * 16 * UNITS // RAW) for s in range(RAW)]
        hi, lo = Signal(sem("hi"), 2 * UNITS), Signal(sem("lo"), 2 * UNITS)
        used = Signal(sem("used"), 2 * UNITS)
        turned = Signal(sem("turned"), 2 * 4)
        x_hi_made, x_lo_made = Signal(sem("x_hi_made"), 2 * 4), Signal(sem("x_lo_made"), 2 * 4)
        gate_first, up_first = Signal(sem("gate_first"), 2 * 4), Signal(sem("up_first"), 2 * 4)
        gate_sum, silued = Signal(sem("gate_sum"), 2 * 4), Signal(sem("silued"), 2 * 4)
        up_sum, product = Signal(sem("up_sum"), 2 * 4), Signal(sem("product"), 2 * 4)
        hid_hi_made, hid_lo_made = Signal(sem("hid_hi_made"), 2 * 4), Signal(sem("hid_lo_made"), 2 * 4)
        scaled_low, scaled_p, scaled_s = (Signal(sem(s), 2 * 2) for s in ("scaled_low", "scaled_p", "scaled_s"))
        indexed = Signal(sem("indexed"), 2 * 2)
        gathered = Signal(sem("gathered"), 2 * 32, ahead=False)
        scattered = Signal(sem("scattered"), 2 * 32, ahead=False)
        written = Signal(sem("written"), 2)

        def half(p, stage):
            first = (p + {"gate": 0, "up": 1, "down": 0, "turn": 1}[stage]) % 2
            return banks[4 * first:4 * first + 4]

        def pair_of_banks(p, stage, b):
            first = 4 * ((p + {"gate": 0, "up": 1}[stage]) % 2) + 2 * b
            both = psum[:, first * BLK:(first + 2) * BLK].rearrange("p (n c) -> p n c", c=BLK)
            return [both[:, :, part * SLOTS:(part + 1) * SLOTS] for part in range(2)]

        def next_of(i, p):
            return (i, 1) if p == 0 else (i + 1, 0)

        def pair_steps(i, last):
            out = []
            after = {Q - 1: ("gate", 0), Q: ("silu", 0), 2 * Q - 1: ("up", 0), 2 * Q: ("high", 0), 2 * Q + 1: ("low", 0),
                     3 * Q - 1: ("gate", 1), 3 * Q: ("silu", 1), 4 * Q - 1: ("up", 1), 4 * Q: ("high", 1), 4 * Q + 1: ("low", 1)}
            for p in range(2):
                for n in range(UNITS):
                    ahead = n + PARTS - 1
                    if ahead < UNITS:
                        out.append(("split", i, p, ahead))
                    elif not (last and p == 1):
                        out.append(("split", *next_of(i, p), ahead - UNITS))
                    out.append(("unit", i, p, n))
                    if n in after:
                        out.append((after[n][0], i, p, after[n][1]))
                    if n == 4 * Q + 2 and not (last and p == 1):
                        out.append(("turn", *next_of(i, p)))
                out.append(("result", i, p))
            return out

        def run(eng, body):
            body("gather", 0, 0)
            body("turn", 0, 0)
            body("gather", 0, 1)
            for n in range(PARTS - 1):
                body("split", 0, 0, n)
            with eng.Fori(0, PAIRS - 1) as i:
                for step in pair_steps(i, False):
                    body(*step)
            for step in pair_steps(PAIRS - 1, True):
                body(*step)

        pair_of_tiles = lambda bank: bank[:, 0:2 * SLOTS].rearrange("p (n c) -> p n c", c=SLOTS)

        with nc.Block() as block:

            @block.sync
            def _(sp):
                start_signals(sp, raw_in)

                def loads(i):
                    for p in range(2):
                        e = sp.snap(2 * i + p)
                        for n in range(UNITS):
                            sp.wait_ge(lo.sem, lo.at(i, p * UNITS + n - RAW))
                            s = n % RAW
                            if n < 4 * Q:
                                w, h = (w_gate, w_up)[n // Q % 2], n // (2 * Q)
                                at = (n % Q) * 2 * P
                                src = w[0, bass.ds(e, 1), at:at + 2 * P, h * BLK:(h + 1) * BLK].rearrange("e (a p) f -> p (e a) f", p=P)
                                to = raw[:, s, :].rearrange("p (a f) -> p a f", f=BLK)
                            else:
                                at = (n - 4 * Q) * P
                                src, to = w_down[0, bass.ds(e, 1), at:at + P, :].rearrange("e p f -> p e f"), raw[:, s:s + 1, :]
                            sp.dma_start(to, src).then_inc(raw_in[s].sem, 16)

                with sp.Fori(0, PAIRS) as i:
                    loads(i)

            @block.tensor
            def _(pe):
                start_signals(pe, [used, turned])

                def body(kind, i, p, n=None):
                    if kind == "turn":
                        pe.wait_ge(gathered.sem, gathered.at(i, 32 * p + 31))
                        pe.wait_ge(product.sem, product.at(i, 4 * p - 1))
                        for b, bank in enumerate(half((p - 1) % 2, "turn")):
                            for k in range(2):
                                at = (2 * b + k) * P
                                pe.transpose(bank[:, k * SLOTS + CAP_PROMPT:(k + 1) * SLOTS], rows_s[:, at:at + P], ident[:])
                                mm = pe.transpose(bank[:, k * SLOTS:k * SLOTS + CAP_PROMPT], rows_p[:, at:at + P],
                                                  ident[0:CAP_PROMPT, 0:CAP_PROMPT])
                            mm.then_inc(turned.sem, 1)
                    elif kind == "unit":
                        s = n % PARTS
                        pe.wait_ge(lo.sem, lo.at(i, p * UNITS + n))
                        if n < 4 * Q:
                            stage, h = ("gate", "up")[n // Q % 2], n // (2 * Q)
                            if n == 0:
                                pe.wait_ge(x_lo_made.sem, x_lo_made.at(i, 4 * p + 3))
                            elif n == Q:
                                pe.wait_ge(scaled_p.sem, scaled_p.at(i, 2 * p - 1))
                                pe.wait_ge(scaled_s.sem, scaled_s.at(i, 2 * p - 1))
                            elif n == 2 * Q:
                                pe.wait_ge(gate_sum.sem, gate_sum.at(i, 4 * p + 1))
                            elif n == 3 * Q:
                                pe.wait_ge(up_sum.sem, up_sum.at(i, 4 * p + 1))
                            for a in range(2):
                                k = 2 * (n % Q) + a
                                for m in range(HALF):
                                    at = slice(a * BLK + m * P, a * BLK + (m + 1) * P)
                                    out = half(p, stage)[m]
                                    pe.matmul(out[:, 0:2 * SLOTS], w_hi[:, s, at], x_parts[:, k, :, :], start=(k == 0),
                                              stop=False, skip_group_check=True)
                                    mm = pe.matmul(out[:, SLOTS:2 * SLOTS], w_lo[:, s, at], x_hi[:, k, :], start=False,
                                                   stop=(k == DT - 1), skip_group_check=True)
                        else:
                            k = n - 4 * Q
                            if k % 2 == 0:
                                pe.wait_ge(hid_lo_made.sem, hid_lo_made.at(i, 4 * p + k // 2))
                            if k == 0:
                                pe.wait_ge(gate_sum.sem, gate_sum.at(i, 4 * p + 3))
                            out = half(p, "down")
                            a, b = hid_hi[sample_slots][:, k, :], hid_lo[:, k, sample_slots]
                            both = hid_both[:, k, :]
                            for h in range(2):
                                u, v = (w[:, s, h * BLK:(h + 1) * BLK] for w in (w_hi, w_lo))
                                first, last = k == 0, k == FT - 1
                                pe.matmul(out[2 + h][:], a, u, start=first, stop=False)
                                pe.matmul(out[2 + h][:], a, v, start=False, stop=False)
                                pe.matmul(out[2 + h][:], b, u, start=False, stop=last)
                                pe.matmul(out[h][:], both, u, start=first, stop=False)
                                mm = pe.matmul(out[h][:], both, v, start=False, stop=last)
                        mm.then_inc(used.sem, 1)

                run(pe, body)

            @block.scalar
            def _(act):
                start_signals(act, [hi, x_hi_made, gate_first, up_first, silued, hid_hi_made, scaled_low, scaled_s])

                def body(kind, i, p, n=None):
                    if kind == "split":
                        s = n % RAW
                        act.wait_ge(raw_in[s].sem, raw_in[s].at(i, 16 * (p * (UNITS // RAW) + n // RAW) + 15))
                        act.wait_ge(used.sem, used.at(i, p * UNITS + n - PARTS))
                        act.copy(w_hi[:, n % PARTS, :], raw[:, s, :]).then_inc(hi.sem, 1)
                    elif kind == "turn":
                        act.wait_ge(used.sem, used.at(i, p * UNITS - FT - 1))
                        for b, bank in enumerate(half((p - 1) % 2, "turn")):
                            act.wait_ge(turned.sem, turned.at(i, 4 * p + b))
                            act.copy(x_hi[:, 2 * b:2 * b + 2, :], pair_of_tiles(bank)).then_inc(x_hi_made.sem, 1)
                    elif kind == "gate":
                        act.wait_ge(used.sem, used.at(i, p * UNITS + (2 * n + 1) * Q - 1))
                        for b in range(2):
                            e = 4 * p + 2 * n + b
                            act.wait_ge(product.sem, product.at(i, e - 4))
                            act.copy(silu[:, 2 * (e % 4):2 * (e % 4) + 2, :], pair_of_banks(p, "gate", b)[0]).then_inc(gate_first.sem, 1)
                    elif kind == "up":
                        act.wait_ge(used.sem, used.at(i, p * UNITS + (2 * n + 2) * Q - 1))
                        for b in range(2):
                            e = 4 * p + 2 * n + b
                            act.wait_ge(hid_lo_made.sem, hid_lo_made.at(i, e - 4))
                            act.copy(hid[:, 2 * (e % 4):2 * (e % 4) + 2, :], pair_of_banks(p, "up", b)[0]).then_inc(up_first.sem, 1)
                    elif kind == "silu":
                        for e in (4 * p + 2 * n, 4 * p + 2 * n + 1):
                            act.wait_ge(gate_sum.sem, gate_sum.at(i, e))
                            part = silu[:, 2 * (e % 4):2 * (e % 4) + 2, :]
                            act.activation(part, part, ACT.Silu).then_inc(silued.sem, 1)
                    elif kind == "high":
                        act.wait_ge(used.sem, used.at(i, p * UNITS - 1))
                        for e in (4 * p + 2 * n, 4 * p + 2 * n + 1):
                            part = (slice(None), slice(2 * (e % 4), 2 * (e % 4) + 2), slice(None))
                            act.wait_ge(product.sem, product.at(i, e))
                            for slots, to in hid_hi.items():
                                made = act.copy(to[part], hid[part][:, :, slots])
                            made.then_inc(hid_hi_made.sem, 1)
                    elif kind == "result":
                        act.wait_ge(used.sem, used.at(i, p * UNITS + UNITS - 1))
                        act.wait_ge(written.sem, written.at(i, p - 1))
                        act.copy(carried_act[:], minus_half[:, 0:1])
                        for h in range(2):
                            act.activation(low_rows[:, h * BLK:(h + 1) * BLK], half(p, "down")[h][CAP_PROMPT:P, :], ACT.Copy,
                                           scale=gate_cols[CAP_PROMPT:P, 0, bass.ds(2 * i + p, 1)]).then_inc(scaled_low.sem, 1)
                        for h in range(2):
                            act.activation(result_s[:, h * BLK:(h + 1) * BLK], half(p, "down")[2 + h][:], ACT.Copy,
                                           scale=gate_cols[:, 1, bass.ds(2 * i + p, 1)]).then_inc(scaled_s.sem, 1)

                run(act, body)

            @block.vector
            def _(dve):
                start_signals(dve, [lo, x_lo_made, gate_sum, up_sum, product, hid_lo_made, scaled_p])

                def body(kind, i, p, n=None):
                    if kind == "split":
                        dve.wait_ge(hi.sem, hi.at(i, p * UNITS + n))
                        dve.tensor_tensor(w_lo[:, n % PARTS, :], raw[:, n % RAW, :], w_hi[:, n % PARTS, :].bitcast(F32),
                                          ALU.subtract).then_inc(lo.sem, 1)
                    elif kind == "turn":
                        for b, bank in enumerate(half((p - 1) % 2, "turn")):
                            dve.wait_ge(x_hi_made.sem, x_hi_made.at(i, 4 * p + b))
                            dve.tensor_tensor(x_lo[:, 2 * b:2 * b + 2, :], pair_of_tiles(bank),
                                              x_hi[:, 2 * b:2 * b + 2, :].bitcast(F32), ALU.subtract).then_inc(x_lo_made.sem, 1)
                    elif kind == "gate":
                        for b in range(2):
                            e = 4 * p + 2 * n + b
                            part = silu[:, 2 * (e % 4):2 * (e % 4) + 2, :]
                            second = pair_of_banks(p, "gate", b)[1]
                            dve.wait_ge(gate_first.sem, gate_first.at(i, e))
                            dve.tensor_tensor(part, part, second, ALU.add).then_inc(gate_sum.sem, 1)
                    elif kind == "up":
                        for b in range(2):
                            e = 4 * p + 2 * n + b
                            part = hid[:, 2 * (e % 4):2 * (e % 4) + 2, :]
                            second = pair_of_banks(p, "up", b)[1]
                            dve.wait_ge(up_first.sem, up_first.at(i, e))
                            dve.tensor_tensor(part, part, second, ALU.add).then_inc(up_sum.sem, 1)
                        for b in range(2):
                            e = 4 * p + 2 * n + b
                            part = (slice(None), slice(2 * (e % 4), 2 * (e % 4) + 2), slice(None))
                            dve.wait_ge(up_sum.sem, up_sum.at(i, e))
                            dve.wait_ge(silued.sem, silued.at(i, e))
                            dve.tensor_tensor(hid[part], hid[part], silu[part], ALU.mult).then_inc(product.sem, 1)
                    elif kind == "low":
                        for e in (4 * p + 2 * n, 4 * p + 2 * n + 1):
                            part = (slice(None), slice(2 * (e % 4), 2 * (e % 4) + 2), slice(None))
                            dve.wait_ge(hid_hi_made.sem, hid_hi_made.at(i, e))
                            for slots, high in hid_hi.items():
                                made = dve.tensor_tensor(hid_lo[part][:, :, slots], hid[part][:, :, slots], high[part].bitcast(F32), ALU.subtract)
                            made.then_inc(hid_lo_made.sem, 1)
                    elif kind == "result":
                        for h in range(2):
                            dve.wait_ge(scaled_low.sem, scaled_low.at(i, 2 * p + h))
                            dve.scalar_tensor_tensor(result_p[:, h * BLK:(h + 1) * BLK], half(p, "down")[h][0:CAP_PROMPT, :],
                                                     gate_cols[0:CAP_PROMPT, 0, bass.ds(2 * i + p, 1)],
                                                     low_rows[:, h * BLK:(h + 1) * BLK], ALU.mult, ALU.add).then_inc(scaled_p.sem, 1)

                run(dve, body)

            @block.gpsimd
            def _(pool):
                start_signals(pool, [indexed, written])
                carry = Carrier(pool, carried_pool, minus_half)

                def body(kind, i, p, n=None):
                    if kind == "gather":
                        pool.wait_ge(turned.sem, turned.at(i, 4 * p - 1))
                        carry()
                        e = bass.ds(2 * i + p, 1)
                        pool.tensor_copy(index_p[:, p:p + 1], index_cols[0:CAP_PROMPT, 0, e]).then_inc(indexed.sem, 1)
                        pool.tensor_copy(index_s[:, p:p + 1], index_cols[:, 1, e]).then_inc(indexed.sem, 1)
                        pool.wait_ge(indexed.sem, indexed.at(i, 2 * p + 1))
                        carry()
                        for rows, index in ((rows_p, index_p), (rows_s, index_s)):
                            pool.indirect_dma_start(rows[:], None, h2_dram, bass.IndirectOffsetOnAxis(ap=index[:, p:p + 1], axis=0)
                                                    ).then_inc(gathered.sem, 16)
                    elif kind == "result":
                        pool.wait_ge(scaled_p.sem, scaled_p.at(i, 2 * p + 1))
                        pool.wait_ge(scaled_s.sem, scaled_s.at(i, 2 * p + 1))
                        carry()
                        for rows, index in ((result_p, index_p), (result_s, index_s)):
                            pool.indirect_dma_start(y_dram, bass.IndirectOffsetOnAxis(ap=index[:, p:p + 1], axis=0), rows[:], None,
                                                    compute_op=ALU.add).then_inc(scattered.sem, 16)
                        pool.wait_ge(scattered.sem, scattered.at(i, 32 * p + 31))
                        pool.sem_inc(written.sem, 1)

                def with_gathers(i, last):
                    for p in range(2):
                        body("result", i, p)
                        if not last:
                            body("gather", i + 1, p)

                body("gather", 0, 0)
                body("gather", 0, 1)
                with pool.Fori(0, PAIRS - 1) as i:
                    with_gathers(i, False)
                with_gathers(PAIRS - 1, True)


def finish(nc, g_final, minus_half, y_dram, out_p, out_s):
    NT = N_TOK // P
    SLOTS_Y = 4
    with ExitStack() as c:
        sem = c.enter_context(semaphores(nc, "f"))
        sb = lambda name, shape: c.enter_context(nc.sbuf_tensor(name, shape, F32))
        y, out, junk, g_row = sb("y", [P, SLOTS_Y, D]), sb("out", [P, SLOTS_Y, D]), sb("junk", [P, D]), sb("g_row", [P, D])
        ss, ms, rstd = sb("ss", [P, NT]), sb("ms", [P, NT]), sb("rstd", [P, NT])
        y_in, y_out = [sem(f"y_in{s}") for s in range(SLOTS_Y)], [sem(f"y_out{s}") for s in range(SLOTS_Y)]
        g_in, squared, mean, powed, normed = sem("g_in"), sem("squared"), sem("mean"), sem("powed"), sem("normed")
        with nc.Block() as block:

            @block.sync
            def _(sp):
                sp.dma_start(g_row[:], g_final.partition_broadcast(P)).then_inc(g_in, 16)
                for t in range(NT):
                    if t >= SLOTS_Y:
                        sp.wait_ge(normed, t - SLOTS_Y + 1)
                    sp.dma_start(y[:, t % SLOTS_Y, :], y_dram[t * P:(t + 1) * P, :]).then_inc(y_in[t % SLOTS_Y], 16)

            @block.scalar
            def _(act):
                def store(t):
                    to = out_s[t * P:(t + 1) * P, :] if t < T_SAMPLE // P else out_p[t * P - T_SAMPLE:(t + 1) * P - T_SAMPLE, :]
                    act.wait_ge(normed, t + 1)
                    act.dma_start(to, out[:, t % SLOTS_Y, :]).then_inc(y_out[t % SLOTS_Y], 16)

                for t in range(NT):
                    act.wait_ge(y_in[t % SLOTS_Y], 16 * (t // SLOTS_Y + 1))
                    if t:
                        act.wait_ge(squared, t)
                    act.activation(junk[:], y[:, t % SLOTS_Y, :], ACT.Square, accum_out=ss[:, t:t + 1]).then_inc(squared, 1)
                    if t >= 2:
                        store(t - 2)
                store(NT - 2)
                store(NT - 1)
                for s in range(SLOTS_Y):
                    act.wait_ge(y_out[s], 16 * (NT // SLOTS_Y))

            @block.gpsimd
            def _(pool):
                for t in range(NT):
                    pool.wait_ge(mean, t + 1)
                    pool.tensor_tensor(rstd[:, t:t + 1], ms[:, t:t + 1], minus_half[:, 0:1], ALU.pow).then_inc(powed, 1)

            @block.vector
            def _(dve):
                dve.wait_ge(g_in, 16)
                for t in range(NT):
                    dve.wait_ge(squared, t + 1)
                    dve.tensor_scalar(ms[:, t:t + 1], ss[:, t:t + 1], 1.0 / D, EPS, ALU.mult, ALU.add).then_inc(mean, 1)
                    dve.wait_ge(powed, t + 1)
                    if t >= SLOTS_Y:
                        dve.wait_ge(y_out[t % SLOTS_Y], 16 * (t // SLOTS_Y))
                    dve.scalar_tensor_tensor(out[:, t % SLOTS_Y, :], y[:, t % SLOTS_Y, :], rstd[:, t:t + 1], g_row[:],
                                             ALU.mult, ALU.mult).then_inc(normed, 1)


def kernel(**inputs):
    import concourse.bacc as bacc
    from concourse.bass_utils import run_bass_kernel_spmd

    a = {name: np.ascontiguousarray(v) for name, v in inputs.items()}
    arrays = {
        "x_s": a["x_sample"].reshape(T_SAMPLE, D), "x_p": a["x_prompt"].reshape(T_PROMPT, D),
        "g_mix": a["norm_mix_g"], "w_in": a["w_in"][0],
        "lq1": a["lambda_q1"], "lk1": a["lambda_k1"], "lq2": a["lambda_q2"], "lk2": a["lambda_k2"],
        "subln": a["diff_subln_g"],
        "lb_cols": np.ascontiguousarray(a["hgrn_lb"].reshape(2 * HEADS, P).T),
        "hg_norm": a["hgrn_norm_g"], "w_out": a["w_out"], "g_ffn": a["norm_ffn_g"],
        "w_router": np.ascontiguousarray(a["w_router"].reshape(DT, P, EXPERTS).transpose(1, 0, 2)),
        "w_gate": a["w_gate"], "w_up": a["w_up"], "w_down": a["w_down"], "g_final": a["final_norm_g"],
        "masks_in": level_masks(), "dist_in": distances(), "ident_in": np.eye(P, dtype=np.float32),
    }
    nc = bacc.Bacc("TRN2", target_bir_lowering=False, num_devices=1)
    args = {n: nc.dram_tensor(f"in_{n}", v.shape, mybir.dt.from_np(v.dtype), kind="ExternalInput").ap()
            for n, v in arrays.items()}
    out_p = nc.dram_tensor("out_prompt", (T_PROMPT, D), F32, kind="ExternalOutput").ap()
    out_s = nc.dram_tensor("out_sample", (T_SAMPLE, D), F32, kind="ExternalOutput").ap()
    build(nc, **args, out_p=out_p, out_s=out_s)
    r = run_bass_kernel_spmd(nc, [{f"in_{n}": v for n, v in arrays.items()}], core_ids=[0]).results[0]
    return r["out_prompt"].reshape(1, T_PROMPT, D), r["out_sample"].reshape(1, T_SAMPLE, D)
```
